# Optimizing a Trainium2 kernel written in Bass

```python
import jax, jax.numpy as jnp
from jax import lax
import numpy as np

D_MODEL = 1024
BATCH = 1
SEQ = 256
DEPTH = 2
DEC_BATCH = 8
DEC_SEQ = 1
PAST_LEN = 1024
PAGE_SIZE = 128

HEAD_DIM = 64
DSWA_GROUPS = ((128, 1), (512, 4), (2048, 16))
HEADS_PER_GROUP = 2
A_HEADS = HEADS_PER_GROUP * len(DSWA_GROUPS)
A_WIDTH = A_HEADS * HEAD_DIM
A_OUT = HEADS_PER_GROUP * HEAD_DIM
CONV_WIDTH = 384
CONV_K = 3
C_HEADS = 4
C_DK = 64
C_DV = 64
C_WIDTH = C_HEADS * C_DK
CHUNK = 64
N_BRANCH = 3
D_FF = 4 * D_MODEL
ROPE_THETA = 10000.0
EPS = 1e-6
NEG_BIG = -1e30
LB_FLOOR = 1e-30
IN_COLS = 3 * A_WIDTH + 3 * CONV_WIDTH + 4 * C_WIDTH + N_BRANCH * D_MODEL

kernel_name = 'hybrid_dilated_conv_hgrn2_step'

def rmsnorm(x, g):
    xf = x.astype(jnp.float32)
    y = xf * lax.rsqrt(jnp.mean(xf * xf, axis=-1, keepdims=True) + EPS)
    return (y * g.astype(jnp.float32)).astype(x.dtype)

def split_in(z):
    sizes = [A_WIDTH] * 3 + [CONV_WIDTH] * 3 + [C_WIDTH] * 4 + [N_BRANCH * D_MODEL]
    idx, acc = [], 0
    for s in sizes[:-1]:
        acc += s
        idx.append(acc)
    return jnp.split(z, idx, axis=-1)

def rope(x, pos):
    half = HEAD_DIM // 2
    inv = ROPE_THETA ** (-jnp.arange(half, dtype=jnp.float32) / half)
    ang = pos.astype(jnp.float32)[:, None] * inv[None, :]
    cos = jnp.cos(ang)[None, :, None, :]
    sin = jnp.sin(ang)[None, :, None, :]
    xf = x.astype(jnp.float32)
    x1, x2 = xf[..., :half], xf[..., half:]
    return jnp.concatenate([x1 * cos - x2 * sin, x2 * cos + x1 * sin], axis=-1).astype(x.dtype)

def masked_softmax(s, valid):
    s = jnp.where(valid, s.astype(jnp.float32) * (HEAD_DIM ** -0.5), NEG_BIG)
    lse = jax.nn.logsumexp(s, axis=-1, keepdims=True)
    return jnp.exp(s - lse), lse[..., 0]

def dilated_band_attn(q, k, v, window, dil):
    bsz, T, H, dh = q.shape
    band = window // dil
    n = T // dil
    nb = -(-n // band)
    n_pad = nb * band

    def by_residue(t, front):
        t = t.reshape(bsz, n, dil, H, dh).transpose(0, 2, 1, 3, 4)
        return jnp.pad(t, ((0, 0), (0, 0), (front, n_pad - n), (0, 0), (0, 0)))

    qb = by_residue(q, 0).reshape(bsz, dil, nb, band, H, dh)
    kb = by_residue(k, band).reshape(bsz, dil, nb + 1, band, H, dh)
    vb = by_residue(v, band).reshape(bsz, dil, nb + 1, band, H, dh)
    kk = jnp.concatenate([kb[:, :, :-1], kb[:, :, 1:]], axis=3)
    vv = jnp.concatenate([vb[:, :, :-1], vb[:, :, 1:]], axis=3)
    s = jnp.einsum('brnqhd,brnkhd->brnhqk', qb, kk)
    qi = jnp.arange(band)[:, None]
    kj = jnp.arange(2 * band)[None, :]
    dist = qi + band - kj
    key_idx = jnp.arange(nb)[:, None, None] * band + kj[None] - band
    valid = (dist >= 0) & (dist <= band) & (key_idx >= 0)
    p, lse = masked_softmax(s, valid[None, None, :, None])
    o = jnp.einsum('brnhqk,brnkhd->brnqhd', p.astype(v.dtype), vv)
    o = o.reshape(bsz, dil, n_pad, H, dh)[:, :, :n].transpose(0, 2, 1, 3, 4).reshape(bsz, T, H, dh)
    lse = lse.transpose(0, 1, 2, 4, 3).reshape(bsz, dil, n_pad, H)[:, :, :n]
    lse = lse.transpose(0, 2, 1, 3).reshape(bsz, T, H)
    return o, lse

def dilated_gather_attn(q, kv_ext, window, dil, pos):
    T = q.shape[1]
    band = window // dil
    steps = jnp.arange(band + 1)
    idx = window + jnp.arange(T)[:, None] - dil * steps[None, :]
    key_pos = pos[:, None] - dil * steps[None, :]
    kv = kv_ext[:, idx]
    s = jnp.einsum('bthd,btkhd->bhtk', q, kv[:, :, :, 0])
    p, lse = masked_softmax(s, (key_pos >= 0)[None, None])
    o = jnp.einsum('bhtk,btkhd->bthd', p.astype(kv.dtype), kv[:, :, :, 1])
    return o, lse.transpose(0, 2, 1)

def hgrn2_chunked(q, log_f, k, v, s0):
    bsz, T, H, dk = q.shape
    dv = v.shape[-1]
    nc = -(-T // CHUNK)
    tp = nc * CHUNK

    def chunks(t):
        t = jnp.pad(t.astype(jnp.float32), ((0, 0), (0, tp - T), (0, 0), (0, 0)))
        return t.reshape(bsz, nc, CHUNK, H, t.shape[-1]).transpose(1, 0, 3, 2, 4)

    qc, bc, kc, vc = chunks(q), jnp.cumsum(chunks(log_f), axis=3), chunks(k), chunks(v)
    causal = jnp.tril(jnp.ones((CHUNK, CHUNK), dtype=bool))

    def step(S, inp):
        qi, bi, ki, vi = inp
        diff = bi[:, :, :, None, :] - bi[:, :, None, :, :]
        decay = jnp.exp(jnp.where(causal[:, :, None], diff, NEG_BIG))
        att = jnp.einsum('bhtc,bhsc,bhtsc->bhts', qi, ki, decay)
        o = jnp.einsum('bhts,bhsv->bhtv', att, vi) + jnp.einsum('bhtc,bhcv->bhtv', qi * jnp.exp(bi), S)
        bl = bi[:, :, -1:, :]
        S = jnp.exp(bl)[:, :, 0, :, None] * S + jnp.einsum('bhsc,bhsv->bhcv', ki * jnp.exp(bl - bi), vi)
        return S, o

    s_fin, o = lax.scan(step, s0.astype(jnp.float32), (qc, bc, kc, vc))
    o = o.transpose(1, 0, 3, 2, 4).reshape(bsz, tp, H, dv)[:, :T]
    return o, s_fin

def trunk_layer(x, pos, kv_prev, conv_prev, hgrn_prev, gather,
                w_in, b_gate, norm1, conv_w, lower, hgrn_norm, w_pa, w_pb, w_pc, w_o, norm2, w_up, w_down):
    bsz, T, _ = x.shape
    h = rmsnorm(x, norm1)
    qa, ka, va, hb, gate_b, gate_c, qc, fc, ic, og, zg = split_in(h @ w_in)

    qa = rope(qa.reshape(bsz, T, A_HEADS, HEAD_DIM), pos)
    ka = rope(ka.reshape(bsz, T, A_HEADS, HEAD_DIM), pos)
    va = va.reshape(bsz, T, A_HEADS, HEAD_DIM)
    outs, lses, new_kv = [], [], []
    for gi, (win, dil) in enumerate(DSWA_GROUPS):
        sl = slice(gi * HEADS_PER_GROUP, (gi + 1) * HEADS_PER_GROUP)
        kv_new = jnp.stack([ka[:, :, sl], va[:, :, sl]], axis=2)
        kv_ext = jnp.concatenate([kv_prev[gi], kv_new], axis=1)
        if gather:
            o_g, lse_g = dilated_gather_attn(qa[:, :, sl], kv_ext, win, dil, pos)
        else:
            o_g, lse_g = dilated_band_attn(qa[:, :, sl], ka[:, :, sl], va[:, :, sl], win, dil)
        outs.append(o_g.astype(jnp.float32))
        lses.append(lse_g)
        new_kv.append(kv_ext[:, -win:])
    wts = jax.nn.softmax(jnp.stack(lses, axis=0), axis=0)
    ya = jnp.sum(wts[..., None] * jnp.stack(outs, axis=0), axis=0)
    ya = ya.reshape(bsz, T, A_OUT).astype(x.dtype)

    u = gate_c * hb
    u_ext = jnp.concatenate([conv_prev, u], axis=1)
    conv = sum(conv_w[j] * u_ext[:, j:j + T] for j in range(CONV_K))
    yb = gate_b * conv
    new_conv = u_ext[:, -(CONV_K - 1):]

    zf = fc.astype(jnp.float32).reshape(bsz, T, C_HEADS, C_DK)
    lb = lower.reshape(C_HEADS, C_DK)
    log_f = jnp.logaddexp(jnp.log(jnp.maximum(lb, LB_FLOOR)), jnp.log1p(-lb) + jax.nn.log_sigmoid(zf))
    kgate = (1.0 - lb) * jax.nn.sigmoid(-zf)
    oc, s_fin = hgrn2_chunked(qc.reshape(bsz, T, C_HEADS, C_DK), log_f, kgate,
                              ic.reshape(bsz, T, C_HEADS, C_DV), hgrn_prev)
    oc = oc * lax.rsqrt(jnp.mean(oc * oc, axis=-1, keepdims=True) + EPS)
    oc = oc * hgrn_norm.astype(jnp.float32).reshape(C_HEADS, C_DV)
    oc = oc * jax.nn.silu(og.astype(jnp.float32).reshape(bsz, T, C_HEADS, C_DV))
    yc = oc.reshape(bsz, T, C_WIDTH).astype(x.dtype)

    g = jax.nn.sigmoid((zg + b_gate).astype(jnp.float32)).reshape(bsz, T, N_BRANCH, D_MODEL)
    mix = g[:, :, 0] * (ya @ w_pa) + g[:, :, 1] * (yb @ w_pb) + g[:, :, 2] * (yc @ w_pc)
    x = x + mix.astype(x.dtype) @ w_o

    h2 = rmsnorm(x, norm2)
    x = x + jnp.square(jax.nn.relu(h2 @ w_up)) @ w_down
    return x, (new_kv[0], new_kv[1], new_kv[2], new_conv, s_fin.astype(x.dtype))

def setup_inputs(seed: int = 0) -> dict:
    key = jax.random.key(seed)
    ks = jax.random.split(key, 24)
    d = D_MODEL

    def nrm(k, shape, scale=1.0):
        return jax.random.normal(k, shape, jnp.float32) * scale

    def kv_shape(win):
        return (DEPTH, DEC_BATCH, win, 2, HEADS_PER_GROUP, HEAD_DIM)

    return {
        'x_prompt': nrm(ks[0], (BATCH, SEQ, d)),
        'x_sample': nrm(ks[1], (DEC_BATCH, DEC_SEQ, d)),
        'cache_kv_w128': nrm(ks[2], kv_shape(DSWA_GROUPS[0][0])),
        'cache_kv_w512': nrm(ks[3], kv_shape(DSWA_GROUPS[1][0])),
        'cache_kv_w2048': nrm(ks[4], kv_shape(DSWA_GROUPS[2][0])),
        'state_conv': nrm(ks[5], (DEPTH, DEC_BATCH, CONV_K - 1, CONV_WIDTH)),
        'state_hgrn': nrm(ks[6], (DEPTH, DEC_BATCH, C_HEADS, C_DK, C_DV), 0.3),
        'w_in': nrm(ks[7], (DEPTH, d, IN_COLS), d ** -0.5),
        'b_gate': nrm(ks[8], (DEPTH, N_BRANCH * d), 0.1),
        'norm1': 1.0 + nrm(ks[9], (DEPTH, d), 0.05),
        'conv_w': nrm(ks[10], (DEPTH, CONV_K, CONV_WIDTH), CONV_K ** -0.5),
        'hgrn_lb': nrm(ks[11], (DEPTH, C_WIDTH), 0.5),
        'hgrn_norm': 1.0 + nrm(ks[12], (DEPTH, C_WIDTH), 0.05),
        'w_pa': nrm(ks[13], (DEPTH, A_OUT, d), A_OUT ** -0.5),
        'w_pb': nrm(ks[14], (DEPTH, CONV_WIDTH, d), CONV_WIDTH ** -0.5),
        'w_pc': nrm(ks[15], (DEPTH, C_WIDTH, d), C_WIDTH ** -0.5),
        'w_o': nrm(ks[16], (DEPTH, d, d), d ** -0.5),
        'norm2': 1.0 + nrm(ks[17], (DEPTH, d), 0.05),
        'w_up': nrm(ks[18], (DEPTH, d, D_FF), d ** -0.5),
        'w_down': nrm(ks[19], (DEPTH, D_FF, d), D_FF ** -0.5),
        'norm_f': 1.0 + nrm(ks[20], (d,), 0.05),
    }

def reference(x_prompt, x_sample, cache_kv_w128, cache_kv_w512, cache_kv_w2048, state_conv, state_hgrn,
              w_in, b_gate, norm1, conv_w, hgrn_lb, hgrn_norm, w_pa, w_pb, w_pc, w_o, norm2, w_up, w_down,
              norm_f):
    sm = jax.nn.softmax(hgrn_lb.astype(jnp.float32), axis=0)
    lower = jnp.cumsum(sm, axis=0) - sm[0:1]
    bp, tp = x_prompt.shape[:2]
    bs, ts = x_sample.shape[:2]
    pos_p = jnp.arange(tp, dtype=jnp.int32)
    pos_s = PAST_LEN + jnp.arange(ts, dtype=jnp.int32)
    caches = (cache_kv_w128, cache_kv_w512, cache_kv_w2048)
    xp, xs = x_prompt, x_sample
    new_p = [[] for _ in range(5)]
    new_s = [[] for _ in range(5)]
    for l in range(DEPTH):
        params = (w_in[l], b_gate[l], norm1[l], conv_w[l], lower[l], hgrn_norm[l], w_pa[l], w_pb[l],
                  w_pc[l], w_o[l], norm2[l], w_up[l], w_down[l])
        zero_kv = [jnp.zeros((bp, win, 2, HEADS_PER_GROUP, HEAD_DIM), xp.dtype) for win, _ in DSWA_GROUPS]
        xp, st_p = trunk_layer(xp, pos_p, zero_kv, jnp.zeros((bp, CONV_K - 1, CONV_WIDTH), xp.dtype),
                               jnp.zeros((bp, C_HEADS, C_DK, C_DV), xp.dtype), False, *params)
        xs, st_s = trunk_layer(xs, pos_s, [c[l] for c in caches], state_conv[l], state_hgrn[l], True, *params)
        for i in range(5):
            new_p[i].append(st_p[i])
            new_s[i].append(st_s[i])
    y_prompt = rmsnorm(xp, norm_f)
    y_sample = rmsnorm(xs, norm_f)
    kvp128, kvp512, kvp2048, conv_p, hgrn_p = [jnp.stack(s, axis=0) for s in new_p]
    kvs128, kvs512, kvs2048, conv_s, hgrn_s = [jnp.stack(s, axis=0) for s in new_s]
    return (y_prompt, y_sample, kvp128, kvp512, kvp2048, conv_p, hgrn_p, kvs128, kvs512, kvs2048, conv_s, hgrn_s)


_drawn_inputs = setup_inputs


def setup_inputs(seed=0):
    import zlib

    import numpy as np

    out = dict(_drawn_inputs(seed))
    spreads = {}
    factors = {'hgrn_norm': 2.861}
    for name, (base, spread) in spreads.items():
        noise = np.random.default_rng([zlib.crc32(name.encode()), seed]).standard_normal(out[name].shape)
        drawn = base * np.exp(spread * noise) if base else spread * noise
        out[name] = __import__('jax').numpy.asarray(drawn.astype(out[name].dtype))
    for name, factor in factors.items():
        out[name] = (out[name] * factor).astype(out[name].dtype)
    return out
```

```python
from contextlib import ExitStack

import numpy as np

import concourse.bass as bass
from concourse import mybir

F32 = mybir.dt.float32
F32R = mybir.dt.float32r
U32 = mybir.dt.uint32
ALU = mybir.AluOpType
ACT = mybir.ActivationFunctionType
AX_X = mybir.AxisListType.X

P = 128
D_MODEL, DEPTH, PROMPT, SAMPLES, PAST = 1024, 2, 256, 8, 1024
TOK = PROMPT + SAMPLES
KT = D_MODEL // P
HD = 64
HALF = P // 2
GROUPS = ((128, 1), (512, 4), (2048, 16))
NG = len(GROUPS)
BAND = 128
D_FF = 4 * D_MODEL
FT = D_FF // P
EPS = 1e-6
LB_FLOOR = 1e-30
NEG = -1e30
SCALE = HD ** -0.5
ROW = 2 * 2 * HD

CT_Q, CT_K, CT_V, CT_HB, CT_GB, CT_GC, CT_CQ, CT_CF, CT_CI, CT_CO, CT_GATE = 0, 3, 6, 9, 12, 15, 18, 20, 22, 24, 26
N_GATE = 24
PAIR_ORDER = [10, 9, 11, 12, 0, 1, 2, 3, 4, 5, 6, 7, 8] + list(range(13, 25))
CT_OF_UNIT = [2 * c + h for c in PAIR_ORDER for h in range(2)]
UNIT_OF_CT = {ct: u for u, ct in enumerate(CT_OF_UNIT)}
BT = 6

U_IN, U_BR, U_O, U_UP, U_DN, UNITS = 0, 50, 58, 66, 98, 130
O_IN, O_O, O_UP, O_DN, OUTS = 0, 50, 58, 90, 98
RING = 4
PAIRS = UNITS // 2
LEVELS = [1, 2, 4, 8, 16, 32, 64, 128]

TURNS = (
    ["norm1"]
    + ["values T", "sample values T"]
    + [f"level {i} {h}" for i in range(3) for h in range(2)]
    + ["rotate 0", "rotate 1", "rotate 2"]
    + [f"level 3 {h}" for h in range(2)]
    + ["sample values 0", "sample values 1"]
    + [f"level 4 {h}" for h in range(2)]
    + ["rotate 3", "rotate 4"]
    + [f"level 5 {h}" for h in range(2)]
    + ["rotate 5"]
    + [f"level {i} {h}" for i in (6, 7) for h in range(2)]
    + ["level 8 0", "level 8 1"]
    + ["recurrence", "decayed keys T", "sample recurrence", "state", "head norm 0", "head norm 1"]
    + [f"kv T {g}" for g in range(NG)]
    + ["sample kv T 0", "sample kv T 1", "sample q T"]
    + ["scores 0 0", "scores 0 1", "scores 0 2"]
    + [f"sample q {b}" for b in range(4)]
    + ["probs T 0 0", "probs T 0 1", "probs T 0 2", "attend 0"]
    + ["scores 1 0", "scores 1 1", "scores 1 2"]
    + [f"sample q {b}" for b in range(4, 8)]
    + ["probs T 1 0", "probs T 1 1", "probs T 1 2", "attend 1"]
    + ["sample scores T", "sample probs T", "sample attend"]
    + [f"branch {m} {j}" for m in range(KT) for j in range(3)]
    + ["norm2"]
)
TURN = {name: i for i, name in enumerate(TURNS)}
BANK_TURNS = [len(TURNS[b::4]) for b in range(4)]
OTHER_SIGNAL = {f"branch {m} 2" for m in range(KT)}
READY_TURNS = [sum(name not in OTHER_SIGNAL for name in TURNS[b::4]) for b in range(4)]
READY_INDEX = {name: sum(t not in OTHER_SIGNAL for t in TURNS[i % 4:i + 1:4]) for name, i in TURN.items()}

DVE_STEPS, ACT_STEPS, POOL_STEPS = 30, 3, 70

C_G1, C_G2, C_BG, C_CW, C_HN, C_LB, C_OM, NPAR = 0, 8, 16, 40, 49, 51, 53, 55
K_ID, K_ROT, K_ONE, K_BLK, K_COS, K_SIN, K_DIAG, K_HSEL = 0, 128, 256, 384, 512, 776, 1040, 1064
NCONST = 1064 + 128


def ring_before(i, n):
    return (3, 4, 1, 2)[i] if i < 4 else i + 1


def trunk(nc, io):
    with ExitStack() as ctx:
        def sb(name, shape, dt=F32, stack=ctx):
            return stack.enter_context(nc.sbuf_tensor(name, shape, dt))

        def sem(name):
            return ctx.enter_context(nc.semaphore(name))

        raw = sb("raw", [P, 2, KT, 2 * P])
        w_hi = sb("w_hi", [P, RING, KT, P], F32R)
        w_lo = sb("w_lo", [P, RING, KT, P], F32R)
        x = sb("x", [P, KT, TOK])
        h_hi = sb("h_hi", [P, KT, TOK], F32R)
        h_lo = sb("h_lo", [P, KT, TOK], F32R)
        consts = sb("consts", [P, NCONST])
        bands = sb("bands", [P, 9 * P])
        levels = sb("levels", [P, P + 7 * HALF])
        par = sb("par", [P, DEPTH, NPAR])
        cur = sb("cur", [P, NPAR])
        hlb = sb("hlb", [P, DEPTH, 2])
        lb_tmp = sb("lb_tmp", [P, 8, 2])
        eps = sb("eps", [P, 1])
        std = sb("std", [P, TOK])
        rstd = sb("rstd", [P, TOK])
        sq = sb("sq", [P, TOK])
        sq_sum = sb("sq_sum", [P, TOK])
        zeros = sb("zeros", [P, 512])
        conv_in = sb("conv_in", [P, 3, 2 + PROMPT])

        with ExitStack() as early:
            gates = sb("gates", [P, N_GATE, TOK], stack=early)
            z = sb("z", [P, CT_GATE, TOK], stack=early)
            kv_tm = sb("kv_tm", [P, 2, NG, 2, P], stack=early)
            kv_s = sb("kv_s", [SAMPLES, NG, 2, P], stack=early)
            q_s = sb("q_s", [SAMPLES, NG, P], stack=early)
            kg = sb("kg", [P, 2, TOK], stack=early)
            v_tm = sb("v_tm", [P, 2, 2, P], stack=early)
            v_s = sb("v_s", [SAMPLES, 2, P], stack=early)
            o_c = sb("o_c", [P, 2, TOK], stack=early)
            y_a = sb("y_a", [P, TOK], stack=early)
            f_s = sb("f_s", [P, 2, SAMPLES], stack=early)
            state_p = sb("state_p", [P, 2, HD], stack=early)
            conv_s = sb("conv_s", [P, 3, SAMPLES, 2], stack=early)
            conv_u = sb("conv_u", [P, 3, SAMPLES], stack=early)
            conv_new = sb("conv_new", [P, 3, SAMPLES, 2], stack=early)
            q_heads = sb("q_heads", [P, NG, SAMPLES, 2], stack=early)
            sc = sb("sc", [P, NG, SAMPLES, 2], stack=early)
            pr_s = sb("pr_s", [P, NG, SAMPLES, 2], stack=early)
            s_rows = sb("s_rows", [2 * SAMPLES, NG * P + NG], stack=early)
            new_sc = sb("new_sc", [2 * SAMPLES, NG, SAMPLES], stack=early)
            s_stat = sb("s_stat", [2 * SAMPLES, 3], stack=early)
            new_pv = sb("new_pv", [P, NG, SAMPLES], stack=early)
            ya_new = sb("ya_new", [P, SAMPLES], stack=early)
            stat = sb("stat", [P, 2, 4], stack=early)
            with ExitStack() as s:
                cum_f = sb("cum_f", [P, 2, PROMPT], stack=s)
                suf_f = sb("suf_f", [P, 2, PROMPT], stack=s)
                q_lv = sb("q_lv", [P, 2, 2, PROMPT], stack=s)
                k_lv = sb("k_lv", [P, 2, 2, PROMPT], stack=s)
                att = sb("att", [P, 2, 4, P], stack=s)
                att_far = sb("att_far", [P, 2, 2, P], stack=s)
                k_tm = sb("k_tm", [P, 2, 2, P], stack=s)
                state_s = sb("state_s", [P, SAMPLES, 2, HD], stack=s)
            with ExitStack() as s:
                v_cache = sb("v_cache", [P, SAMPLES, NG, P], stack=s)
                probs = sb("probs", [P, 9 * P], stack=s)
                probs_t = sb("probs_t", [P, 9, P], stack=s)
            sb("shared_region", [P, 48 * P], stack=early)
            with ExitStack() as s:
                k_cache = sb("k_cache", [P, SAMPLES, NG, P], stack=s)
            y_hi = sb("y_hi", [P, BT, TOK], F32R, stack=early)
            y_lo = sb("y_lo", [P, BT, TOK], F32R, stack=early)
        with ExitStack() as s:
            sb("gates_below", [P, N_GATE, TOK], stack=s)
            mix_hi = sb("mix_hi", [P, KT, TOK], F32R, stack=s)
            mix_lo = sb("mix_lo", [P, KT, TOK], F32R, stack=s)
            gated = sb("gated", [P, 2, 3, TOK], stack=s)
            mix = sb("mix", [P, 2, TOK], stack=s)
        a_hi = sb("a_hi", [P, FT, TOK], F32R)
        a_lo = sb("a_lo", [P, FT, TOK], F32R)
        u_relu = sb("u_relu", [P, RING, TOK])
        a_full = sb("a_full", [P, RING, TOK])
        kv_outer = gates[:, 0:4, :].rearrange("p a t -> p (a t)")[:, 0:SAMPLES * 2 * HD].rearrange(
            "p (b h v) -> p b h v", b=SAMPLES, h=2)
        rope_sin = gates[:, 4:10, :]

        ident = consts[:, K_ID:K_ID + P]
        rot = consts[:, K_ROT:K_ROT + P]
        ones = consts[:, K_ONE:K_ONE + P]
        blk = consts[:, K_BLK:K_BLK + P]
        cos = consts[:, K_COS:K_COS + TOK]
        sin = consts[:, K_SIN:K_SIN + TOK]
        diag = consts[0:16, K_DIAG:K_DIAG + 24]
        hsel = consts[0:16, K_HSEL:K_HSEL + P]

        main = [ctx.enter_context(nc.psum_tensor(f"main{i}", [P, 512], F32)) for i in range(4)]
        small = [ctx.enter_context(nc.psum_tensor(f"small{i}", [P, 512], F32)) for i in range(4)]

        gain_in, x_in = sem("gain_in"), [sem("x_in0"), sem("x_in1")]
        params_in, consts_in = sem("params_in"), sem("consts_in")
        levels_in, bands_in = sem("levels_in"), sem("bands_in")
        raw_landed = [sem("raw_landed0"), sem("raw_landed1")]
        w_hi_ready = sem("w_hi_ready")
        w_lo_ready = sem("w_lo_ready")
        w_used = sem("w_used")
        out_taken = sem("out_taken")
        bank_ready = [sem(f"bank_ready{b}") for b in range(4)]
        bank_taken = [sem(f"bank_taken{b}") for b in range(4)]
        dve_step, act_step, pool_step = sem("dve_step"), sem("act_step"), sem("pool_step")
        pool_setup = sem("pool_setup")
        layer_params = sem("layer_params")
        h_hi_ready = sem("h_hi_ready")
        h_ready = sem("h_ready")
        sq_ready = sem("sq_ready")
        std_ready = sem("std_ready")
        setup_done = sem("setup_done")
        lb_ready, lb_exp, lb_step = sem("lb_ready"), sem("lb_exp"), sem("lb_step")
        sigmoids = sem("sigmoids")
        decays = sem("decays")
        kg_ready = sem("kg_ready")
        att_clear = sem("att_clear")
        v_tm_ready = sem("v_tm_ready")
        v_s_ready = sem("v_s_ready")
        level_ready = sem("level_ready")
        level_used = sem("level_used")
        masked = sem("masked")
        far_ready = sem("far_ready")
        outer_ready = sem("outer_ready")
        state_s_ready = sem("state_s_ready")
        state_s_used = sem("state_s_used")
        state_in = sem("state_in")
        final_keys = sem("final_keys")
        k_tm_ready = sem("k_tm_ready")
        state_p_ready = sem("state_p_ready")
        o_ready = sem("o_ready")
        o_sq_ready = sem("o_sq_ready")
        o_std = sem("o_std")
        silu_ready = sem("silu_ready")
        o_scaled = sem("o_scaled")
        o_inv = sem("o_inv")
        yc_ready = sem("yc_ready")
        sin_ready = sem("sin_ready")
        roped = sem("roped")
        conv_in_ready = sem("conv_in_ready")
        conv_out = sem("conv_out")
        yb_ready = sem("yb_ready")
        conv_new_ready = sem("conv_new_ready")
        kv_tm_ready = sem("kv_tm_ready")
        kv_s_ready = sem("kv_s_ready")
        q_s_ready = sem("q_s_ready")
        q_heads_ready = sem("q_heads_ready")
        keys_in, values_in = sem("keys_in"), sem("values_in")
        keys_clear = sem("keys_clear")
        scored = sem("scored")
        maxed = sem("maxed")
        exped = sem("exped")
        probs_ready = sem("probs_ready")
        probs_t_ready = sem("probs_t_ready")
        attended = sem("attended")
        s_scored, s_rows_ready, s_exped = sem("s_scored"), sem("s_rows_ready"), sem("s_exped")
        s_probs, s_probs_t = sem("s_probs"), sem("s_probs_t")
        ya_ready = sem("ya_ready")
        y_hi_ready, y_ready = sem("y_hi_ready"), sem("y_ready")
        gates_ready = sem("gates_ready")
        gated_ready = sem("gated_ready")
        mix_ready, mix_hi_ready, mix_lo_ready = sem("mix_ready"), sem("mix_hi_ready"), sem("mix_lo_ready")
        u_used = sem("u_used")
        a_hi_ready, a_ready = sem("a_hi_ready"), sem("a_ready")
        states_stored = sem("states_stored")
        stored = sem("stored")
        shifted = sem("shifted")
        y_out = sem("y_out")

        waits_over = sem("waits_over")

        def use_bank(pe, l, name):
            i = TURN[name]
            pe.wait_ge(bank_taken[i % 4], l * BANK_TURNS[i % 4] + i // 4 + 1)
            return small[i % 4]

        def done(ins, name):
            ins.then_inc(bank_ready[TURN[name] % 4], 1)

        def take(eng, l, name):
            b = TURN[name] % 4
            eng.wait_ge(bank_ready[b], l * READY_TURNS[b] + READY_INDEX[name])
            return small[b]

        def taken(ins, name):
            ins.then_inc(bank_taken[TURN[name] % 4], 1)

        def after_taken(eng, l, name):
            i = TURN[name]
            eng.wait_ge(bank_taken[i % 4], l * BANK_TURNS[i % 4] + i // 4 + 2)

        def wait_ends(eng):
            eng.sem_inc(waits_over, 1)

        def unit_done(eng, l, u):
            eng.wait_ge(w_used, l * UNITS + 4 + u + 1)

        def z_ready(eng, l, ct):
            eng.wait_ge(out_taken, l * OUTS + 4 + UNIT_OF_CT[ct] + 1)

        def x_ready(eng, l, n, m=KT - 1):
            eng.wait_ge(out_taken, l * OUTS + 4 + (0, O_O + m + 1, O_DN + m + 1)[n])

        def stepper(eng, semaphore, l, total):
            count = [0]

            def step(ins):
                count[0] += 1
                ins.then_inc(semaphore, 1)
                eng.wait_ge(semaphore, l * total + count[0])

            def check():
                assert count[0] == total, (semaphore, count[0])
            return step, check

        def raw_of(u, k=KT):
            return raw[:, (u // 2) % 2, 0:k, (u % 2) * P:(u % 2) * P + P]

        STORES, STATE_STORES = 10, 6
        SHIFTS = 37

        block = ctx.enter_context(nc.Block())

        @block.sync
        def _(sp):
            sp.dma_start(cur[:, C_G1:C_G1 + KT], io["gain0"]).then_inc(gain_in, 16)
            for i in range(2):
                ks = slice(i * KT // 2, (i + 1) * KT // 2)
                sp.dma_start(x[:, ks, :], io["xT"].rearrange("(k p) t -> p k t", p=P)[:, ks, :]).then_inc(x_in[i], 16)
            sp.dma_start(par[:, :, 0:C_LB], io["params"]).then_inc(params_in, 16)
            sp.dma_start(hlb[:, :, :], io["hlb"]).then_inc(params_in, 16)

            def weights(l, p, src, first, k=KT):
                sp.wait_ge(w_lo_ready, first)
                wait_ends(sp)
                sp.dma_start(raw[:, p % 2, 0:k, :], src).then_inc(raw_landed[p % 2], 16)

            def w_in_pair(l, col):
                return io["w_in"][bass.ds(l, 1), :, bass.ds(col, 2 * P)].rearrange("a (k p) n -> p (a k) n", p=P)

            def before(l, p):
                return l * UNITS + ((4, 2)[p] if p < 2 else 2 * p + 2)

            def store(dst, src, signal=stored):
                sp.dma_start(dst, src).then_inc(signal, 16)

            def shift(l, g, b, first, rows):
                win = GROUPS[g][0]
                n = 16 if rows % 16 == 0 else rows
                src = io[f"cache{g}"][bass.ds(l, 1), bass.ds(b, 1), first + 1:first + 1 + rows]
                dst = io[f"kvs{g}"][bass.ds(l, 1), bass.ds(b, 1), first:first + rows]
                assert first + rows <= win - 1
                sp.dma_start(dst.rearrange("l b (n r) c -> (l b n) (r c)", n=n),
                             src.rearrange("l b (n r) c -> (l b n) (r c)", n=n)).then_inc(shifted, 16)

            sp.sem_inc(stored, 16)
            sp.sem_inc(states_stored, 16)
            sp.wait_ge(setup_done, 1)
            with sp.Fori(0, DEPTH) as l:
                for p in range(25):
                    weights(l, p, w_in_pair(l, PAIR_ORDER[p] * 2 * P), before(l, p))
                    if p == 2:
                        unit_done(sp, l, 0)
                        sp.wait_ge(states_stored, l * STATE_STORES * 16 + 16)
                        hg = io["state_hgrn"][bass.ds(l, 1)].rearrange("l b (hp h) c v -> h hp c (l b) v", h=2)
                        for h in range(2):
                            for hp in range(2):
                                sp.dma_start(state_s[h * HD:(h + 1) * HD, :, hp, :], hg[h, hp]).then_inc(state_in, 16)
                        sp.dma_start(conv_s[:, :, :, :], io["state_convT"][bass.ds(l, 1)].rearrange(
                            "l p j b s -> (l p) j b s")).then_inc(state_in, 16)
                    if p == 4:
                        for g, (win, dil) in enumerate(GROUPS):
                            n = min(BAND, PAST // dil)
                            rows = io[f"cache{g}"][bass.ds(l, 1)].rearrange("l b (n d) c -> n (l b) d c", d=dil)
                            sp.dma_start(k_cache[0:n, :, g, :], rows[BAND - n:BAND, :, 0, 0:P]).then_inc(keys_in, 16)
                    if 5 <= p < 13:
                        shift(l, 1, p - 5, 0, 496)
                    if p == 13:
                        sp.wait_ge(state_s_used, l + 1)
                        hg = io["hgs"][bass.ds(l, 1)].rearrange("l b (hp h) c v -> h hp c (l b) v", h=2)
                        for h in range(2):
                            for hp in range(2):
                                store(hg[h, hp], state_s[h * HD:(h + 1) * HD, :, hp, :], states_stored)
                    if p == 14:
                        sp.wait_ge(state_p_ready, l + 1)
                        wait_ends(sp)
                        hg = io["hgp"][bass.ds(l, 1)].rearrange("l b (hp h) c v -> h c (l b hp) v", h=2)
                        for h in range(2):
                            store(hg[h], state_p[h * HD:(h + 1) * HD, :, :], states_stored)
                    if p == 15:
                        sp.wait_ge(kv_tm_ready, l * NG + NG)
                        wait_ends(sp)
                        for g, (win, dil) in enumerate(GROUPS):
                            for tb in range(2) if win > BAND else (1,):
                                r = max(win, PROMPT) - PROMPT + tb * P - (PROMPT - win if win < PROMPT else 0)
                                store(io[f"kvp{g}"][bass.ds(l, 1), 0, r:r + P].rearrange("l r c -> (l r) c"),
                                      kv_tm[:, tb, g, :, :].rearrange("p a c -> p (a c)"))
                        sp.wait_ge(kv_s_ready, l * 2 + 2)
                        for g, (win, dil) in enumerate(GROUPS):
                            store(io[f"kvs{g}"][bass.ds(l, 1), :, win - 1].rearrange("l b c -> (l b) c"),
                                  kv_s[:, g, :, :].rearrange("p a c -> p (a c)"))
                    if p == 16:
                        sp.wait_ge(o_ready, 2 * l + 2)
                        wait_ends(sp)
                        sp.wait_ge(state_p_ready, l + 1)
                        wait_ends(sp)
                        sp.wait_ge(states_stored, l * STATE_STORES * 16 + 16 + STATE_STORES * 16)
                        for g, (win, dil) in enumerate(GROUPS):
                            n = min(BAND, PAST // dil)
                            rows = io[f"cache{g}"][bass.ds(l, 1)].rearrange("l b (n d) c -> n (l b) d c", d=dil)
                            sp.dma_start(v_cache[0:n, :, g, :], rows[BAND - n:BAND, :, 0, P:2 * P]).then_inc(
                                values_in, 16)
                    if p == 17:
                        sp.wait_ge(conv_new_ready, l + 1)
                        store(io["convsT"][bass.ds(l, 1)].rearrange("l p j b s -> (l p) (j b s)"),
                              conv_new[:, :, :, :].rearrange("p j b s -> p (j b s)"))
                        store(io["convpT"][bass.ds(l, 1)].rearrange("l p j s -> (l p) j s"),
                              conv_in[:, :, PROMPT:PROMPT + 2])
                    if p == 18:
                        for g, (win, dil) in enumerate(GROUPS):
                            if win > PROMPT:
                                n = (win - PROMPT) * ROW // (P * 512)
                                sp.dma_start(
                                    io[f"kvp{g}"][bass.ds(l, 1), 0, 0:win - PROMPT].rearrange(
                                        "l (p r) c -> (l p) (r c)", p=P).rearrange("p (n c) -> p n c", n=n),
                                    zeros[:, :].unsqueeze(1).to_broadcast([P, n, 512])).then_inc(shifted, 16)
                    if p == 19:
                        for g, first in ((0, 112), (1, 496), (2, 2032)):
                            sp.dma_start(
                                io[f"kvs{g}"][bass.ds(l, 1), :, first:first + 15].rearrange("l b r c -> (l b) (r c)"),
                                io[f"cache{g}"][bass.ds(l, 1), :, first + 1:first + 16].rearrange(
                                    "l b r c -> (l b) (r c)")).then_inc(shifted, 16)
                    if 20 <= p < 24:
                        shift(l, 0, 2 * (p - 20), 0, 112)
                        shift(l, 0, 2 * (p - 20) + 1, 0, 112)
                for i in range(4):
                    p = U_BR // 2 + i
                    weights(l, p, io["w_br"][bass.ds(l, 1), :, i * 2 * P:(i + 1) * 2 * P].rearrange(
                        "a (k p) n -> p (a k) n", p=P), before(l, p), k=BT)
                for i in range(4):
                    p = U_O // 2 + i
                    weights(l, p, io["w_o"][bass.ds(l, 1), :, i * 2 * P:(i + 1) * 2 * P].rearrange(
                        "a (k p) n -> p (a k) n", p=P), before(l, p))
                with sp.Fori(0, FT // 4) as i:
                    for j in range(2):
                        p = U_UP // 2 + j
                        weights(l, p, io["w_up"][bass.ds(l, 1), :, bass.ds(i * 512 + j * 2 * P, 2 * P)].rearrange(
                            "a (k p) n -> p (a k) n", p=P), l * UNITS + i * 4 + 2 * p + 2)
                    shift(l, 2, i, 0, 1024)
                with sp.Fori(0, 4) as i:
                    for kc in range(4):
                        p = U_DN // 2 + kc
                        weights(l, p, io["w_down"][bass.ds(l, 1), kc * D_MODEL:(kc + 1) * D_MODEL,
                                                   bass.ds(i * 2 * P, 2 * P)].rearrange(
                            "a (k p) n -> p (a k) n", p=P), l * UNITS + i * 8 + 2 * p + 2)
                        if kc % 2:
                            shift(l, 2, i * 2 + kc // 2, 1024, 1008)
            sp.wait_ge(y_out, KT)
            store(io["yT"].rearrange("(k p) t -> p k t", p=P), x[:, :, :])
            sp.wait_ge(stored, 16 + DEPTH * STORES * 16 + 16)
            sp.wait_ge(states_stored, 16 + DEPTH * STATE_STORES * 16)
            sp.wait_ge(shifted, DEPTH * SHIFTS * 16)

        @block.tensor
        def _(pe):
            def unit(slot, out, rhs_hi, rhs_lo, k0, nk, wk0=0, start=True, stop=True, per_k=None):
                for k in range(nk):
                    if per_k is not None:
                        per_k(k)
                    wh, wl = w_hi[:, slot, wk0 + k, :], w_lo[:, slot, wk0 + k, :]
                    rh, rl = rhs_hi[:, k0 + k, :], rhs_lo[:, k0 + k, :]
                    pe.matmul(out[:, 0:TOK], wh, rh, start=start and k == 0, stop=False)
                    pe.matmul(out[:, 0:TOK], wh, rl, start=False, stop=False)
                    last = pe.matmul(out[:, 0:TOK], wl, rh, start=False, stop=stop and k == nk - 1)
                return last

            def sum_squares(l, name, n):
                pe.wait_ge(sq_ready, l * 2 + n + 1)
                bank = use_bank(pe, l, name)
                done(pe.matmul(bank[:, 0:TOK], ones, sq_sum[:, :], start=True, stop=True), name)

            def transposes(l, name, parts):
                bank = use_bank(pe, l, name)
                for col, src in parts:
                    k, n = src.shape[0], src.size() // src.shape[0]
                    mm = pe.transpose(bank[0:n, col:col + k], src, ident[0:k, 0:k])
                done(mm, name)

            def level(l, i):
                if i:
                    pe.wait_ge(level_ready, l * 8 + i)
                else:
                    pe.wait_ge(kg_ready, l + 1)
                    z_ready(pe, l, CT_CQ + 1)

                def operands(hp, h):
                    rows = slice(h * HD, (h + 1) * HD)
                    if i:
                        return k_lv[rows, i % 2, hp, :], q_lv[rows, i % 2, hp, :]
                    return kg[rows, hp, 0:PROMPT], z[rows, CT_CQ + hp, 0:PROMPT]

                def queries(qq, tb):
                    if not i:
                        return qq[:, tb * P:tb * P + P]
                    return qq[:, tb * P:tb * P + P].rearrange("p (n s t) -> p n s t", s=2, t=LEVELS[i - 1])[:, :, 1, :]
                w = HALF if i else P
                for h in range(2):
                    bank = use_bank(pe, l, f"level {i} {h}")
                    for hp in range(2):
                        kk, qq = operands(hp, h)
                        if i == 8:
                            c = hp * P
                            mm = pe.matmul(bank[:, c:c + P], kk[:, 0:P], qq[:, P:2 * P], start=True, stop=True)
                            continue
                        for tb in range(2):
                            c = (hp * 2 + tb) * w
                            mm = pe.matmul(bank[:, c:c + w], kk[:, tb * P:tb * P + P], queries(qq, tb),
                                           start=True, stop=True)
                    done(mm, f"level {i} {h}")

            def rotate(l, ct):
                z_ready(pe, l, ct)
                bank = use_bank(pe, l, f"rotate {ct}")
                done(pe.matmul(bank[:, 0:TOK], rot, z[:, ct, :], start=True, stop=True), f"rotate {ct}")

            def scores(l, h):
                rows = slice(h * HD, (h + 1) * HD)
                bank = use_bank(pe, l, f"scores {h} 0")
                for g in range(NG):
                    mm = pe.matmul(bank[:, g * P:g * P + P], z[rows, CT_Q + g, 0:P], z[rows, CT_K + g, 0:P],
                                   start=True, stop=True)
                done(mm, f"scores {h} 0")
                for j, gs in ((1, (0, 1)), (2, (2,))):
                    bank = use_bank(pe, l, f"scores {h} {j}")
                    for n, g in enumerate(gs):
                        mm = pe.matmul(bank[:, n * PROMPT:(n + 1) * PROMPT], z[rows, CT_Q + g, P:2 * P],
                                       z[rows, CT_K + g, 0:PROMPT], start=True, stop=True)
                    done(mm, f"scores {h} {j}")

            def sample_q(l, b):
                bank = use_bank(pe, l, f"sample q {b}")
                done(pe.matmul(bank[:, 0:NG * P], ident[0:SAMPLES, b:b + 1].to_broadcast([SAMPLES, P]),
                               q_s[:, :, :].rearrange("p g c -> p (g c)"), start=True, stop=True), f"sample q {b}")

            def attend(l, h):
                pe.wait_ge(probs_t_ready, l * 6 + h * 3 + 3)
                name = f"attend {h}"
                bank = use_bank(pe, l, name)
                rows = slice(h * HD, (h + 1) * HD)
                for g in range(NG):
                    pe.matmul(bank[rows, 0:P], kv_tm[:, 0, g, 1, rows], probs_t[:, g, :], start=g == 0, stop=g == NG - 1)
                for g in range(NG):
                    for tb in range(2):
                        mm = pe.matmul(bank[rows, P:2 * P], kv_tm[:, tb, g, 1, rows], probs_t[:, NG + 2 * g + tb, :],
                                       start=g == 0 and tb == 0, stop=g == NG - 1 and tb == 1)
                done(mm, name)

            def between(l, u):
                if u == 0:
                    pe.wait_ge(consts_in, 16)
                    sum_squares(l, "norm1", 0)
                if u == 7:
                    z_ready(pe, l, CT_CI + 1)
                    transposes(l, "values T", [((tb * 2 + hp) * P, z[:, CT_CI + hp, tb * P:tb * P + P])
                                               for tb in range(2) for hp in range(2)])
                    transposes(l, "sample values T", [(hp * P, z[:, CT_CI + hp, PROMPT:TOK]) for hp in range(2)])
                for at, i in ((8, 0), (9, 1), (11, 2), (13, 3), (15, 4), (16, 5), (18, 6), (20, 7), (21, 8)):
                    if u == at:
                        level(l, i)
                    if u == 12 and at == 11:
                        for ct in range(3):
                            rotate(l, ct)
                    if u == 14 and at == 13:
                        pe.wait_ge(v_s_ready, l + 1)
                        for i4 in range(2):
                            name = f"sample values {i4}"
                            bank = use_bank(pe, l, name)
                            for bb in range(4):
                                for h in range(2):
                                    rows = slice(h * HD, (h + 1) * HD)
                                    b = i4 * 4 + bb
                                    mm = pe.matmul(bank[rows, bb * P:bb * P + P],
                                                   ident[0:SAMPLES, b:b + 1].to_broadcast([SAMPLES, HD]),
                                                   v_s[:, :, rows], start=True, stop=True)
                            done(mm, name)
                    if u == at == 15:
                        rotate(l, 3)
                        rotate(l, 4)
                    if u == at == 16:
                        rotate(l, 5)
                if u == 23:
                    pe.wait_ge(masked, l * 16 + 16)
                    pe.wait_ge(far_ready, 2 * l + 2)
                    pe.wait_ge(v_tm_ready, l + 1)
                    bank = use_bank(pe, l, "recurrence")
                    for hp in range(2):
                        for h in range(2):
                            rows = slice(h * HD, (h + 1) * HD)
                            c = hp * PROMPT
                            pe.matmul(bank[rows, c:c + P], v_tm[:, 0, hp, rows], att[:, h, hp * 2, :],
                                      start=True, stop=True)
                            pe.matmul(bank[rows, c + P:c + 2 * P], v_tm[:, 0, hp, rows], att_far[:, h, hp, :],
                                      start=True, stop=False)
                            mm = pe.matmul(bank[rows, c + P:c + 2 * P], v_tm[:, 1, hp, rows], att[:, h, hp * 2 + 1, :],
                                           start=False, stop=True)
                    done(mm, "recurrence")
                    pe.wait_ge(final_keys, l + 1)
                    transposes(l, "decayed keys T", [((tb * 2 + hp) * P, q_lv[:, 1, hp, tb * P:tb * P + P])
                                                     for tb in range(2) for hp in range(2)])
                if u == 24:
                    pe.wait_ge(state_s_ready, l + 1)
                    bank = use_bank(pe, l, "sample recurrence")
                    wait_ends(pe)
                    for hp in range(2):
                        for b in range(SAMPLES):
                            for h in range(2):
                                rows = slice(h * HD, (h + 1) * HD)
                                mm = pe.matmul(bank[rows, hp * SAMPLES + b:hp * SAMPLES + b + 1],
                                               state_s[rows, b, hp, :], z[rows, CT_CQ + hp, PROMPT + b:PROMPT + b + 1],
                                               start=True, stop=True)
                    done(mm, "sample recurrence")
                    pe.wait_ge(k_tm_ready, l + 1)
                    bank = use_bank(pe, l, "state")
                    for hp in range(2):
                        for h in range(2):
                            rows = slice(h * HD, (h + 1) * HD)
                            for tb in range(2):
                                mm = pe.matmul(bank[rows, hp * HD:(hp + 1) * HD], k_tm[:, tb, hp, rows],
                                               v_tm[:, tb, hp, rows], start=tb == 0, stop=tb == 1)
                    done(mm, "state")
                if u == 25:
                    pe.wait_ge(o_sq_ready, l + 1)
                    for hp in range(2):
                        bank = use_bank(pe, l, f"head norm {hp}")
                        done(pe.matmul(bank[:, 0:TOK], blk, z[:, CT_CF + hp, :], start=True, stop=True),
                             f"head norm {hp}")
                if u == 26:
                    pe.wait_ge(roped, l * 6 + 6)
                    for g in range(NG):
                        transposes(l, f"kv T {g}", [((tb * 2 + kv) * P, z[:, (CT_K, CT_V)[kv] + g, tb * P:tb * P + P])
                                                    for tb in range(2) for kv in range(2)])
                    kvs = [z[:, (CT_K, CT_V)[kv] + g, PROMPT:TOK] for g in range(NG) for kv in range(2)]
                    transposes(l, "sample kv T 0", [(i * P, s) for i, s in enumerate(kvs[0:4])])
                    transposes(l, "sample kv T 1", [(i * P, s) for i, s in enumerate(kvs[4:6])])
                    transposes(l, "sample q T", [(g * P, z[:, CT_Q + g, PROMPT:TOK]) for g in range(NG)])
                for h in range(2):
                    if u == 27 + 5 * h:
                        scores(l, h)
                    if u in (28 + 5 * h, 29 + 5 * h):
                        pe.wait_ge(q_s_ready, l + 1)
                        for b in range(2):
                            sample_q(l, 4 * h + 2 * (u - 28 - 5 * h) + b)
                    if u == 30 + 5 * h:
                        pe.wait_ge(probs_ready, l * 2 + h + 1)
                        for j in range(3):
                            transposes(l, f"probs T {h} {j}", [((b % 4) * P, probs[:, b * P:b * P + P])
                                                              for b in range(4 * j, min(4 * j + 4, 9))])
                    if u == 31 + 5 * h:
                        pe.wait_ge(kv_tm_ready, l * NG + NG)
                        attend(l, h)
                if u == 39:
                    pe.wait_ge(s_scored, l + 1)
                    pe.wait_ge(q_heads_ready, l + 1)
                    name = "sample scores T"
                    bank = use_bank(pe, l, name)
                    for g in range(NG):
                        pe.transpose(bank[0:16, g * P:g * P + P], sc[:, g, :, :].rearrange("p b h -> p (b h)"), ident)
                    for g in range(NG):
                        c = NG * P + g * SAMPLES
                        mm = pe.matmul(bank[0:16, c:c + SAMPLES], q_heads[:, g, :, :].rearrange("p b h -> p (b h)"),
                                       z[:, CT_K + g, PROMPT:TOK], start=True, stop=True)
                    done(mm, name)
                if u == 41:
                    pe.wait_ge(s_probs, l + 1)
                    name = "sample probs T"
                    bank = use_bank(pe, l, name)
                    for g in range(NG):
                        wait_ends(pe)
                        pe.transpose(bank[:, g * 16:g * 16 + 16], s_rows[:, g * P:g * P + P], ident[0:16, 0:16])
                    done(pe.matmul(bank[:, 64:64 + NG * SAMPLES], hsel, new_sc[:, :, :].rearrange("p g b -> p (g b)"),
                                   start=True, stop=True), name)
                if u == 42:
                    pe.wait_ge(s_probs_t, l + 1)
                    pe.wait_ge(values_in, l * NG * 16 + NG * 16)
                    name = "sample attend"
                    bank = use_bank(pe, l, name)
                    for b in range(SAMPLES):
                        for g, (win, dil) in enumerate(GROUPS):
                            n = min(BAND, PAST // dil)
                            mm = pe.matmul(bank[:, 2 * b:2 * b + 2], v_cache[0:n, b, g, :], pr_s[0:n, g, b, :],
                                           start=g == 0, stop=g == NG - 1)
                    done(mm, name)

            pe.sem_inc(w_used, 4)
            for b in range(4):
                pe.sem_inc(bank_taken[b], 1)

            with pe.Fori(0, DEPTH) as l:
                for u in range(50):
                    pe.wait_ge(w_lo_ready, l * UNITS + u + 5)
                    pe.wait_ge(out_taken, l * OUTS + ring_before(u, OUTS))
                    per_k = (lambda k: pe.wait_ge(h_ready, l * 2 * KT + k + 1)) if u == 0 else None
                    unit(u % 4, main[u % 4], h_hi, h_lo, 0, KT, per_k=per_k).then_inc(w_used, 1)
                    between(l, u)

                for m in range(KT):
                    u = U_BR + m
                    pe.wait_ge(w_lo_ready, l * UNITS + u + 5)
                    if m == 0:
                        pe.wait_ge(y_ready, l * 3 + 3)
                    for j, (k0, nk) in enumerate(((0, 1), (1, 3), (4, 2))):
                        bank = use_bank(pe, l, f"branch {m} {j}")
                        mm = unit(u % 4, bank, y_hi, y_lo, k0, nk, wk0=k0)
                        if j < 2:
                            done(mm, f"branch {m} {j}")
                    mm.then_inc(w_used, 1)
                for m in range(KT):
                    u = U_O + m
                    pe.wait_ge(w_lo_ready, l * UNITS + u + 5)
                    pe.wait_ge(out_taken, l * OUTS + O_O + m + 1)
                    per_k = (lambda k: pe.wait_ge(mix_lo_ready, l * KT + k + 1)) if m == 0 else None
                    unit(u % 4, main[(O_O + m) % 4], mix_hi, mix_lo, 0, KT, per_k=per_k).then_inc(w_used, 1)
                for j in range(4):
                    u = U_UP + j
                    pe.wait_ge(w_lo_ready, l * UNITS + u + 5)
                    pe.wait_ge(out_taken, l * OUTS + O_UP + j + 1)
                    per_k = (lambda k: pe.wait_ge(h_ready, l * 2 * KT + KT + k + 1)) if j == 0 else None
                    unit(u % 4, main[(O_UP + j) % 4], h_hi, h_lo, 0, KT, per_k=per_k).then_inc(w_used, 1)
                    if j == 0:
                        sum_squares(l, "norm2", 1)
                with pe.Fori(1, FT // 4) as i:
                    for j in range(4):
                        pe.wait_ge(w_lo_ready, l * UNITS + i * 4 + U_UP + j + 5)
                        pe.wait_ge(out_taken, l * OUTS + i * 4 + O_UP + j + 1)
                        unit((U_UP + j) % 4, main[(O_UP + j) % 4], h_hi, h_lo, 0, KT).then_inc(w_used, 1)
                with pe.Fori(0, 2) as i:
                    for mp in range(2):
                        for kc in range(4):
                            for h in range(2):
                                n = mp * 8 + kc * 2 + h
                                m = mp * 2 + h
                                pe.wait_ge(w_lo_ready, l * UNITS + i * 16 + U_DN + n + 5)
                                if kc == 0:
                                    pe.wait_ge(out_taken, l * OUTS + i * 4 + O_DN + m + 1)
                                if h == 0:
                                    pe.wait_ge(a_ready, l * FT + kc * KT + KT + 4)
                                unit((U_DN + n) % 4, main[(O_DN + m) % 4], a_hi, a_lo, kc * KT, KT,
                                     start=kc == 0, stop=kc == 3).then_inc(w_used, 1)
            sum_squares(DEPTH, "norm1", 0)

        @block.scalar
        def _(act):
            def split_hi(l, u, k=KT, need=None, landed=None):
                n = 33 - (u // 2) % 2
                act.wait_ge(raw_landed[(u // 2) % 2], (l * n + u // 4 + 1) * 16 if landed is None else landed)
                act.wait_ge(w_used, l * UNITS + ring_before(u, UNITS) if need is None else need)
                act.activation(w_hi[:, u % 4, 0:k, :], raw_of(u, k), ACT.Copy).then_inc(w_hi_ready, 1)

            def norm_hi(l, n, k):
                x_ready(act, l, n, k)
                g = (C_G1, C_G2, C_G1)[n]
                act.activation(h_hi[:, k, :], x[:, k, :], ACT.Copy, scale=cur[:, g + k:g + k + 1]).then_inc(h_hi_ready, 1)

            def norm_std(l, n):
                name = ("norm1", "norm2")[n]
                bank = take(act, l, name)
                act.activation(std[:, :], bank[:, 0:TOK], ACT.Sqrt, bias=eps[:, 0:1],
                               scale=1.0 / D_MODEL).then_inc(std_ready, 1)
                act.wait_ge(std_ready, l * 2 + n + 1)
                act.sem_inc(bank_taken[TURN[name] % 4], 1)

            def copy_bank(l, name, dst, src_of, signal):
                bank = take(act, l, name)
                act.activation(dst, src_of(bank), ACT.Copy).then_inc(signal, 1)

            act.wait_ge(setup_done, 1)
            act.wait_ge(gain_in, 16)
            for k in range(KT - 2):
                act.wait_ge(x_in[k // (KT // 2)], 16)
                act.activation(h_hi[:, k, :], x[:, k, :], ACT.Copy, scale=cur[:, C_G1 + k:C_G1 + k + 1])\
                   .then_inc(h_hi_ready, 1)
            act.dma_start(consts[:, :], io["consts"]).then_inc(consts_in, 16)
            act.dma_start(levels[:, :], io["levels"]).then_inc(levels_in, 16)
            act.dma_start(bands[:, :], io["bands"]).then_inc(bands_in, 16)
            act.wait_ge(lb_ready, 1)
            act.activation(lb_tmp[:, 1:1 + DEPTH, :], lb_tmp[:, 1:1 + DEPTH, :], ACT.Exp).then_inc(lb_exp, 1)

            with act.Fori(0, DEPTH) as l:
                step, check_steps = stepper(act, act_step, l, ACT_STEPS)

                def freed(name, signal, value):
                    act.wait_ge(signal, value)
                    act.sem_inc(bank_taken[TURN[name] % 4], 1)

                split_hi(l, 0)
                for k in (KT - 2, KT - 1):
                    norm_hi(l, 0, k)
                for u in range(1, 4):
                    split_hi(l, u)
                act.wait_ge(layer_params, l + 1)
                norm_std(l, 0)
                for u in range(50):
                    if u == 2:
                        z_ready(act, l, CT_CF + 1)
                        step(act.activation(kg[:, :, :], z[:, CT_CF:CT_CF + 2, :], ACT.Sigmoid, scale=-1.0))
                        act.activation(z[:, CT_CF:CT_CF + 2, :], z[:, CT_CF:CT_CF + 2, :], ACT.Sigmoid)\
                           .then_inc(sigmoids, 1)
                    if u == 8:
                        z_ready(act, l, CT_CO + 1)
                        act.activation(o_c[:, :, :], z[:, CT_CO:CT_CO + 2, :], ACT.Sigmoid).then_inc(sigmoids, 1)
                        copy_bank(l, "values T", v_tm[:, :, :, :].rearrange("p t h c -> p (t h c)"),
                                  lambda b: b[:, :], v_tm_ready)
                        freed("values T", v_tm_ready, l + 1)
                        copy_bank(l, "sample values T", v_s[:, :, :].rearrange("p h c -> p (h c)"),
                                  lambda b: b[0:SAMPLES, 0:2 * P], v_s_ready)
                        freed("sample values T", v_s_ready, l + 1)
                    if u == 22:
                        for h in range(2):
                            copy_bank(l, f"level 8 {h}", att_far[:, h, :, :].rearrange("p a c -> p (a c)"),
                                      lambda b: b[:, 0:2 * P], far_ready)
                            freed(f"level 8 {h}", far_ready, 2 * l + h + 1)
                    if u == 24:
                        copy_bank(l, "decayed keys T", k_tm[:, :, :, :].rearrange("p t h c -> p (t h c)"),
                                  lambda b: b[:, :], k_tm_ready)
                        freed("decayed keys T", k_tm_ready, l + 1)
                    if u == 25:
                        act.wait_ge(states_stored, l * STATE_STORES * 16 + 16)
                        copy_bank(l, "state", state_p[:, :, :].rearrange("p h c -> p (h c)"),
                                  lambda b: b[:, 0:2 * HD], state_p_ready)
                        freed("state", state_p_ready, l + 1)
                    if u == 26:
                        for hp in range(2):
                            copy = f"head norm {hp}"
                            bank = take(act, l, copy)
                            act.activation(z[:, CT_CI + hp, :], bank[:, 0:TOK], ACT.Sqrt, bias=eps[:, 0:1])\
                               .then_inc(o_std, 1)
                            freed(copy, o_std, 2 * l + hp + 1)
                    if u == 27:
                        act.wait_ge(stored, l * STORES * 16 + 16)
                        for g in range(NG):
                            copy_bank(l, f"kv T {g}", kv_tm[:, :, g, :, :],
                                      lambda b: b[:, :].rearrange("p (t k c) -> p t k c", t=2, k=2), kv_tm_ready)
                            freed(f"kv T {g}", kv_tm_ready, NG * l + g + 1)
                        for i, gs in ((0, slice(0, 2)), (1, slice(2, 3))):
                            n = 2 * P * (gs.stop - gs.start)
                            copy_bank(l, f"sample kv T {i}", kv_s[:, gs, :, :].rearrange("p g k c -> p (g k c)"),
                                      lambda b: b[0:SAMPLES, 0:n], kv_s_ready)
                            freed(f"sample kv T {i}", kv_s_ready, 2 * l + i + 1)
                        copy_bank(l, "sample q T", q_s[:, :, :].rearrange("p g c -> p (g c)"),
                                  lambda b: b[0:SAMPLES, 0:NG * P], q_s_ready)
                        freed("sample q T", q_s_ready, l + 1)
                    for h in range(2):
                        if u == 29 + 5 * h:
                            act.wait_ge(maxed, l * 2 + h + 1)
                            step(act.activation(probs[:, 0:NG * P], probs[:, 0:NG * P], ACT.Exp,
                                                bias=stat[:, h, 0:1], accum_out=stat[:, h, 2:3]))
                            act.activation(probs[:, NG * P:9 * P], probs[:, NG * P:9 * P], ACT.Exp,
                                           bias=stat[:, h, 1:2], accum_out=stat[:, h, 3:4]).then_inc(exped, 1)
                        if u == 31 + 5 * h:
                            for j in range(3):
                                nb = min(4, 9 - 4 * j)
                                if h == 1 and j == 0:
                                    take(act, l, "attend 0")
                                copy_bank(l, f"probs T {h} {j}",
                                          probs_t[:, 4 * j:4 * j + nb, :].rearrange("p b c -> p (b c)"),
                                          lambda b: b[:, 0:nb * P], probs_t_ready)
                                freed(f"probs T {h} {j}", probs_t_ready, l * 6 + h * 3 + j + 1)
                    if u == 40:
                        act.wait_ge(s_rows_ready, l + 1)
                        act.activation(s_rows[:, :], s_rows[:, :], ACT.Exp, bias=s_stat[:, 0:1],
                                       accum_out=s_stat[:, 1:2]).then_inc(s_exped, 1)
                        act.wait_ge(yb_ready, l + 1)
                        act.activation(y_hi[:, 1:4, :], z[:, CT_GB:CT_GB + 3, :], ACT.Copy).then_inc(y_hi_ready, 1)
                        act.wait_ge(yc_ready, 2 * l + 2)
                        act.activation(y_hi[:, 4:6, :], o_c[:, :, :], ACT.Copy).then_inc(y_hi_ready, 1)
                    for g in (range(18) if u == 43 else (u - 26,) if u >= 44 else ()):
                        act.wait_ge(out_taken, l * OUTS + 4 + 26 + g + 1)
                        act.activation(gates[:, g, :], gates[:, g, :], ACT.Sigmoid,
                                       bias=cur[:, C_BG + g:C_BG + g + 1]).then_inc(gates_ready, 1)
                    if u == 44:
                        act.wait_ge(ya_ready, l * 3 + 3)
                        act.activation(y_hi[:, 0, :], y_a[:, :], ACT.Copy).then_inc(y_hi_ready, 1)
                    split_hi(l, u + 4, BT if u + 4 >= U_BR else KT)

                for m in range(KT):
                    u = U_BR + m
                    act.wait_ge(mix_ready, l * KT + m + 1)
                    act.activation(mix_hi[:, m, :], mix[:, m % 2, :], ACT.Copy).then_inc(mix_hi_ready, 1)
                    split_hi(l, u + 4, BT if u + 4 < U_O else KT)
                for m in range(KT):
                    norm_hi(l, 1, m)
                    split_hi(l, U_O + m + 4)
                norm_std(l, 1)
                with act.Fori(0, FT // 4) as i:
                    for j in range(4):
                        act.wait_ge(out_taken, l * OUTS + i * 4 + 4 + O_UP + j + 1)
                        act.wait_ge(a_ready, l * FT + i * 4 + j + 1)
                        act.activation(a_full[:, j, :], u_relu[:, j, :], ACT.Square).then_inc(u_used, 1)
                        act.wait_ge(u_used, l * FT + i * 4 + j + 5)
                        act.activation(a_hi[:, bass.ds(i * 4 + j, 1), :].rearrange("p a t -> p (a t)"),
                                       a_full[:, j, :], ACT.Copy).then_inc(a_hi_ready, 1)
                        v = U_UP + j + 4
                        split_hi(l, v, need=l * UNITS + i * 4 + v + 1,
                                 landed=(l * (33 - (v // 2) % 2) + i + v // 4 + 1) * 16)
                for u in range(U_DN, UNITS):
                    if u + 4 < UNITS:
                        split_hi(l, u + 4)
                    n = u - U_DN
                    if n % 8 >= 6 and n < FT - 2:
                        norm_hi(l, 2, n // 8 * 2 + n % 2)
                check_steps()
            norm_std(DEPTH, 0)

        @block.vector
        def _(dve):
            def split_lo(l, u, k=KT, ready=None):
                dve.wait_ge(w_hi_ready, l * UNITS + u + 1 if ready is None else ready)
                dve.tensor_tensor(w_lo[:, u % 4, 0:k, :], raw_of(u, k), w_hi[:, u % 4, 0:k, :].bitcast(F32),
                                  ALU.subtract).then_inc(w_lo_ready, 1)

            def norm_lo(l, n, k):
                g = (C_G1, C_G2, C_G1)[n]
                dve.wait_ge(h_hi_ready, l * 2 * KT + n * KT + k + 1)
                dve.scalar_tensor_tensor(h_lo[:, k, :], x[:, k, :], cur[:, g + k:g + k + 1],
                                         h_hi[:, k, :].bitcast(F32), ALU.mult, ALU.subtract).then_inc(h_ready, 1)

            def evacuate(l, u):
                unit_done(dve, l, u)
                ct = CT_OF_UNIT[u]
                dst = z[:, ct, :] if ct < CT_GATE else gates[:, ct - CT_GATE, :]
                dve.tensor_tensor(dst, main[u % 4][:, 0:TOK], rstd[:, :], ALU.mult).then_inc(out_taken, 1)

            dve.memset(zeros[:, :], 0.0)
            dve.memset(conv_in[:, :, 0:2], 0.0)
            dve.memset(eps[:, :], EPS).then_inc(setup_done, 1)
            dve.sem_inc(w_lo_ready, 4)
            dve.sem_inc(a_ready, 4)
            for k in range(KT - 2):
                norm_lo(0, 0, k)
            dve.wait_ge(x_in[0], 16)
            dve.wait_ge(x_in[1], 16)
            dve.sem_inc(out_taken, 4)
            dve.wait_ge(params_in, 32)
            dve.tensor_tensor(lb_tmp[:, 0, :], hlb[:, 0, :], hlb[:, 1, :], ALU.max).then_inc(lb_step, 1)
            dve.wait_ge(lb_step, 1)
            for d in range(DEPTH):
                ins = dve.tensor_tensor(lb_tmp[:, 1 + d, :], hlb[:, d, :], lb_tmp[:, 0, :], ALU.subtract)
            ins.then_inc(lb_ready, 1)
            dve.wait_ge(lb_exp, 1)
            dve.tensor_tensor(lb_tmp[:, 3, :], lb_tmp[:, 1, :], lb_tmp[:, 2, :], ALU.add).then_inc(lb_step, 1)
            dve.wait_ge(lb_step, 2)
            dve.reciprocal(lb_tmp[:, 4, :], lb_tmp[:, 3, :]).then_inc(lb_step, 1)
            dve.wait_ge(lb_step, 3)
            for d in range(DEPTH):
                ins = dve.tensor_tensor(lb_tmp[:, 1 + d, :], lb_tmp[:, 1 + d, :], lb_tmp[:, 4, :], ALU.mult)
            ins.then_inc(lb_step, 1)
            dve.wait_ge(lb_step, 4)
            dve.tensor_tensor(lb_tmp[:, 5, :], lb_tmp[:, 1, :], lb_tmp[:, 1, :], ALU.subtract)
            dve.tensor_tensor(lb_tmp[:, 3, :], lb_tmp[:, 1, :], lb_tmp[:, 2, :], ALU.add).then_inc(lb_step, 1)
            dve.wait_ge(lb_step, 5)
            dve.tensor_tensor(lb_tmp[:, 6, :], lb_tmp[:, 3, :], lb_tmp[:, 1, :], ALU.subtract).then_inc(lb_step, 1)
            dve.wait_ge(lb_step, 6)
            for d in range(DEPTH):
                dve.tensor_scalar(par[:, d, C_LB:C_LB + 2], lb_tmp[:, 5 + d, :], LB_FLOOR, None, ALU.max)
                ins = dve.tensor_scalar(par[:, d, C_OM:C_OM + 2], lb_tmp[:, 5 + d, :], -1.0, 1.0, ALU.mult, ALU.add)
            ins.then_inc(lb_step, 1)
            dve.wait_ge(lb_step, 7)

            with dve.Fori(0, DEPTH) as l:
                step, check_steps = stepper(dve, dve_step, l, DVE_STEPS)

                def norm_inverse(n):
                    dve.wait_ge(std_ready, l * 2 + n + 1)
                    step(dve.reciprocal(rstd[:, :], std[:, :]))

                def mask_level(i):
                    if i == 0:
                        dve.wait_ge(levels_in, 16)
                        dve.wait_ge(att_clear, l + 1)
                    for h in range(2):
                        name = f"level {i} {h}"
                        bank = take(dve, l, name)
                        wait_ends(dve)
                        if i:
                            half = LEVELS[i - 1]
                            n, c = HALF // half, P + (i - 1) * HALF
                            dst = att[:, h, :, :].rearrange("p a (n s t) -> p a n s t", s=2, t=half)[:, :, :, 1, :]
                            mask = levels[:, c:c + HALF].rearrange("p (n t) -> p n t", n=n)
                            src = bank[:, 0:4 * HALF].rearrange("p (a n t) -> p a n t", a=4, n=n)
                            mask = mask.unsqueeze(1).to_broadcast([P, 4, n, half])
                        else:
                            dst, mask = att[:, h, :, :], levels[:, 0:P].unsqueeze(1).to_broadcast([P, 4, P])
                            src = bank[:, :].rearrange("p (a c) -> p a c", a=4)
                        ins = dve.copy_predicated(dst, mask.bitcast(U32), src)
                        ins.then_inc(masked, 1)
                        dve.wait_ge(masked, l * 16 + 2 * i + h + 1)
                        dve.sem_inc(bank_taken[TURN[name] % 4], 1)

                def rope(ct):
                    name = f"rotate {ct}"
                    bank = take(dve, l, name)
                    dve.tensor_tensor(rope_sin[:, ct, :], bank[:, 0:TOK], sin, ALU.mult).then_inc(sin_ready, 1)
                    dve.wait_ge(sin_ready, l * 6 + ct + 1)
                    dve.sem_inc(bank_taken[TURN[name] % 4], 1)

                def mask_scores(h):
                    if h == 0:
                        dve.wait_ge(bands_in, 16)
                    if h == 1:
                        take(dve, l, "probs T 0 2")
                    at = 0
                    for j, n in enumerate((NG * P, 2 * PROMPT, PROMPT)):
                        bank = take(dve, l, f"scores {h} {j}")
                        taken_step(dve.scalar_tensor_tensor(probs[:, at:at + n], bank[:, 0:n], SCALE,
                                                            bands[:, at:at + n], ALU.mult, ALU.add),
                                   f"scores {h} {j}")
                        at += n
                    dve.reduce_max(stat[:, h, 0:1], probs[:, 0:NG * P], AX_X, negate=True)
                    dve.reduce_max(stat[:, h, 1:2], probs[:, NG * P:9 * P], AX_X, negate=True).then_inc(maxed, 1)

                def taken_step(ins, name):
                    step(ins)
                    dve.sem_inc(bank_taken[TURN[name] % 4], 1)

                def normalise(h):
                    dve.wait_ge(exped, l * 2 + h + 1)
                    step(dve.reciprocal(stat[:, h, 0:2], stat[:, h, 2:4]))
                    dve.tensor_scalar(probs[:, 0:NG * P], probs[:, 0:NG * P], stat[:, h, 0:1], None, ALU.mult)
                    dve.tensor_scalar(probs[:, NG * P:9 * P], probs[:, NG * P:9 * P], stat[:, h, 1:2], None,
                                      ALU.mult).then_inc(probs_ready, 1)

                def sample_products(b):
                    bank = take(dve, l, f"sample q {b}")
                    if b == 0:
                        dve.wait_ge(keys_in, l * NG * 16 + NG * 16)
                    for g in range(NG):
                        n = min(BAND, PAST // GROUPS[g][1])
                        ins = dve.tensor_tensor(k_cache[0:n, b, g, :], k_cache[0:n, b, g, :],
                                                bank[0:n, g * P:g * P + P], ALU.mult)
                    taken_step(ins, f"sample q {b}")

                def convolve():
                    dve.wait_ge(conv_in_ready, l + 1)
                    dve.wait_ge(state_in, (l * 5 + 5) * 16)
                    for tap in (2, 1, 0):
                        for j in range(3):
                            w = cur[:, C_CW + tap * 3 + j:C_CW + tap * 3 + j + 1]
                            acc, acc_s = z[:, CT_GC + j, 0:PROMPT], z[:, CT_GC + j, PROMPT:TOK]
                            src = conv_in[:, j, tap:tap + PROMPT]
                            src_s = conv_u[:, j, :] if tap == 2 else conv_s[:, j, :, tap]
                            if tap == 2:
                                dve.tensor_scalar(acc, src, w, None, ALU.mult)
                                ins = dve.tensor_scalar(acc_s, src_s, w, None, ALU.mult)
                            else:
                                dve.scalar_tensor_tensor(acc, src, w, acc, ALU.mult, ALU.add)
                                ins = dve.scalar_tensor_tensor(acc_s, src_s, w, acc_s, ALU.mult, ALU.add)
                        if tap:
                            step(ins)
                    ins.then_inc(conv_out, 1)

                split_lo(l, 0)
                for k in (KT - 2, KT - 1):
                    norm_lo(l, 0, k)
                dve.wait_ge(h_ready, l * 2 * KT + KT)
                step(dve.tensor_copy(cur[:, :], par[:, bass.ds(l, 1), :].rearrange("p a c -> p (a c)")))
                dve.sem_inc(layer_params, 1)
                for u in range(1, 3):
                    split_lo(l, u)
                norm_inverse(0)
                for u in range(50):
                    if u == 26:
                        dve.wait_ge(state_s_ready, l + 1)
                        dve.wait_ge(roped, l * 6 + 6)
                    evacuate(l, u)
                    if u == 3:
                        dve.wait_ge(sigmoids, 2 * l + 1)
                        for hp in range(2):
                            lb, om = cur[:, C_LB + hp:C_LB + hp + 1], cur[:, C_OM + hp:C_OM + hp + 1]
                            sg = z[:, CT_CF + hp, :]
                            dve.tensor_scalar(cum_f[:, hp, :], sg[:, 0:PROMPT], om, lb, ALU.mult, ALU.add)
                            dve.tensor_scalar(f_s[:, hp, :], sg[:, PROMPT:TOK], om, lb, ALU.mult, ALU.add)
                            ins = dve.tensor_scalar(kg[:, hp, :], kg[:, hp, :], om, None, ALU.mult)
                        step(ins)
                        dve.sem_inc(decays, 1)
                        dve.sem_inc(kg_ready, 1)
                    for at, i in ((9, 0), (10, 1), (12, 2), (14, 3), (16, 4), (17, 5), (19, 6), (21, 7)):
                        if u == at:
                            mask_level(i)
                        if u == 13 and at == 12:
                            for ct in range(3):
                                rope(ct)
                        if u == 15 and at == 14:
                            for i4 in range(2):
                                bank = take(dve, l, f"sample values {i4}")
                                b4 = slice(i4 * 4, i4 * 4 + 4)
                                ks = kg[:, :, PROMPT + i4 * 4:PROMPT + i4 * 4 + 4].rearrange("p h b -> p b h")
                                ins = dve.tensor_tensor(
                                    kv_outer[:, b4, :, :],
                                    bank[:, :].rearrange("p (b h v) -> p b h v", b=4, h=2),
                                    ks.unsqueeze(3).to_broadcast([P, 4, 2, HD]), ALU.mult)
                                ins.then_inc(outer_ready, 1)
                                dve.wait_ge(outer_ready, l * 2 + i4 + 1)
                                dve.sem_inc(bank_taken[TURN[f"sample values {i4}"] % 4], 1)
                        if u == at == 16:
                            rope(3)
                            rope(4)
                        if u == at == 17:
                            rope(5)
                    if u == 24:
                        bank = take(dve, l, "recurrence")
                        dve.wait_ge(silu_ready, l + 1)
                        dve.tensor_copy(o_c[:, :, 0:PROMPT], bank[:, :].rearrange("p (h t) -> p h t", h=2))\
                           .then_inc(o_ready, 1)
                        dve.wait_ge(o_ready, 2 * l + 1)
                        dve.sem_inc(bank_taken[TURN["recurrence"] % 4], 1)
                        bank = take(dve, l, "sample recurrence")
                        dve.tensor_copy(o_c[:, :, PROMPT:TOK],
                                        bank[:, 0:2 * SAMPLES].rearrange("p (h t) -> p h t", h=2)).then_inc(o_ready, 1)
                        dve.wait_ge(o_ready, 2 * l + 2)
                        dve.sem_inc(bank_taken[TURN["sample recurrence"] % 4], 1)
                        dve.sem_inc(state_s_used, 1)
                    if u == 26:
                        dve.wait_ge(o_std, 2 * l + 2)
                        dve.reciprocal(z[:, CT_CI:CT_CI + 2, :], z[:, CT_CI:CT_CI + 2, :]).then_inc(o_inv, 1)
                    if u == 27:
                        convolve()
                    if u == 28:
                        dve.wait_ge(o_scaled, l + 1)
                        for hp in range(2):
                            dve.scalar_tensor_tensor(o_c[:, hp, :], o_c[:, hp, :],
                                                     cur[:, C_HN + hp:C_HN + hp + 1], z[:, CT_CO + hp, :],
                                                     ALU.mult, ALU.mult).then_inc(yc_ready, 1)
                    for h in range(2):
                        if u == 28 + 5 * h:
                            mask_scores(h)
                        if u in (29 + 5 * h, 30 + 5 * h):
                            for b in range(2):
                                sample_products(4 * h + 2 * (u - 29 - 5 * h) + b)
                        if u == 30 + 5 * h:
                            normalise(h)
                        if u == 32 + 5 * h:
                            bank = take(dve, l, f"attend {h}")
                            rows = slice(h * HD, (h + 1) * HD)
                            dve.tensor_copy(y_a[rows, 0:PROMPT], bank[rows, 0:PROMPT]).then_inc(ya_ready, 1)
                            dve.wait_ge(ya_ready, 3 * l + h + 1)
                            dve.sem_inc(bank_taken[TURN[f"attend {h}"] % 4], 1)
                    if u == 38:
                        for g, (win, dil) in enumerate(GROUPS):
                            n = min(BAND, PAST // dil)
                            if n < BAND:
                                dve.memset(sc[n:BAND, g, :, :], NEG / SCALE)
                            ins = dve.tensor_reduce(
                                sc[0:n, g, :, :],
                                k_cache[0:n, :, g, :].rearrange("p b (h d) -> p b h d", h=2), AX_X, ALU.add)
                        ins.then_inc(s_scored, 1)
                    if u == 40:
                        bank = take(dve, l, "sample scores T")
                        dve.tensor_scalar(s_rows[:, 0:NG * P], bank[0:16, 0:NG * P], SCALE, None, ALU.mult)
                        step(dve.scalar_tensor_tensor(
                            new_sc[:, :, :].rearrange("p g b -> p (g b)"), bank[0:16, NG * P:NG * P + NG * SAMPLES],
                            SCALE, diag, ALU.mult, ALU.mult))
                        dve.sem_inc(bank_taken[TURN["sample scores T"] % 4], 1)
                        step(dve.reduce_sum(s_rows[:, NG * P:NG * P + NG], new_sc[:, :, :], AX_X))
                        dve.reduce_max(s_stat[:, 0:1], s_rows[:, :], AX_X, negate=True).then_inc(s_rows_ready, 1)
                        dve.wait_ge(s_exped, l + 1)
                        step(dve.reciprocal(s_stat[:, 2:3], s_stat[:, 1:2]))
                        step(dve.tensor_scalar(s_rows[:, :], s_rows[:, :], s_stat[:, 2:3], None, ALU.mult))
                        dve.tensor_tensor(new_sc[:, :, :], diag.rearrange("p (g b) -> p g b", g=NG),
                                          s_rows[:, NG * P:NG * P + NG].unsqueeze(2).to_broadcast([16, NG, SAMPLES]),
                                          ALU.mult).then_inc(s_probs, 1)
                        for i, (lo_, n) in enumerate(((1, 3), (4, 2))):
                            dve.wait_ge(y_hi_ready, 3 * l + i + 1)
                            src = z[:, CT_GB:CT_GB + 3, :] if i == 0 else o_c[:, :, :]
                            dve.tensor_tensor(y_lo[:, lo_:lo_ + n, :], src, y_hi[:, lo_:lo_ + n, :].bitcast(F32),
                                              ALU.subtract).then_inc(y_ready, 1)
                    if u == 41:
                        bank = take(dve, l, "sample probs T")
                        step(dve.tensor_copy(pr_s[:, :, :, :].rearrange("p g b h -> p (g b h)"), bank[:, 0:48]))
                        dve.sem_inc(s_probs_t, 1)
                        step(dve.tensor_tensor(new_pv[:, :, :],
                                               bank[:, 64:64 + NG * SAMPLES].rearrange("p (g b) -> p g b", g=NG),
                                               z[:, CT_V:CT_V + NG, PROMPT:TOK], ALU.mult))
                        dve.sem_inc(bank_taken[TURN["sample probs T"] % 4], 1)
                        step(dve.reduce_sum(ya_new[:, :], new_pv[:, :, :].rearrange("p g b -> p b g"), AX_X))
                    if u == 42:
                        bank = take(dve, l, "sample attend")
                        for h in range(2):
                            rows = slice(h * HD, (h + 1) * HD)
                            own = bank[rows, 0:16].rearrange("p (b h) -> p b h", h=2)[:, :, h]
                            ins = dve.tensor_tensor(y_a[rows, PROMPT:TOK], own, ya_new[rows, :], ALU.add)
                        step(ins)
                        dve.sem_inc(bank_taken[TURN["sample attend"] % 4], 1)
                        dve.sem_inc(ya_ready, 1)
                    if u == 45:
                        dve.wait_ge(y_hi_ready, 3 * l + 3)
                        dve.tensor_tensor(y_lo[:, 0, :], y_a[:, :], y_hi[:, 0, :].bitcast(F32), ALU.subtract)\
                           .then_inc(y_ready, 1)
                    split_lo(l, u + 3, BT if u + 3 >= U_BR else KT)

                def mix_half(m):
                    dve.wait_ge(mix_hi_ready, l * KT + m + 1)
                    dve.tensor_tensor(mix_lo[:, m, :], mix[:, m % 2, :], mix_hi[:, m, :].bitcast(F32),
                                      ALU.subtract).then_inc(mix_lo_ready, 1)
                for m in range(KT):
                    u = U_BR + m
                    if m >= 2:
                        dve.wait_ge(mix_ready, l * KT + m - 1)
                    dve.wait_ge(gates_ready, l * N_GATE + 2 * KT + m + 1)
                    for j in range(3):
                        name = f"branch {m} {j}"
                        if j < 2:
                            bank = take(dve, l, name)
                        else:
                            unit_done(dve, l, u)
                            bank = small[TURN[name] % 4]
                        dve.tensor_tensor(gated[:, m % 2, j, :], bank[:, 0:TOK], gates[:, j * KT + m, :], ALU.mult)\
                           .then_inc(bank_taken[TURN[name] % 4], 1)
                    split_lo(l, u + 3, BT if u + 3 < U_O else KT)
                    if m:
                        mix_half(m - 1)
                mix_half(KT - 1)
                for m in range(KT):
                    u = U_O + m
                    unit_done(dve, l, u)
                    dve.tensor_tensor(x[:, m, :], main[(O_O + m) % 4][:, 0:TOK], x[:, m, :], ALU.add)\
                       .then_inc(out_taken, 1)
                    split_lo(l, u + 3)
                    norm_lo(l, 1, m)
                norm_inverse(1)
                wait_ends(dve)
                with dve.Fori(0, FT // 4) as i:
                    for j in range(4):
                        dve.wait_ge(w_used, l * UNITS + i * 4 + 4 + U_UP + j + 1)
                        dve.wait_ge(u_used, l * FT + i * 4 + j + 1)
                        dve.scalar_tensor_tensor(u_relu[:, j, :], main[(O_UP + j) % 4][:, 0:TOK], 0.0, rstd[:, :],
                                                 ALU.max, ALU.mult).then_inc(out_taken, 1)
                        v = U_UP + j + 3
                        split_lo(l, v, ready=l * UNITS + i * 4 + v + 1)
                        dve.wait_ge(a_hi_ready, l * FT + i * 4 + j + 1)
                        at = bass.ds(i * 4 + j, 1)
                        dve.tensor_tensor(a_lo[:, at, :].rearrange("p a t -> p (a t)"), a_full[:, j, :],
                                          a_hi[:, at, :].rearrange("p a t -> p (a t)").bitcast(F32),
                                          ALU.subtract).then_inc(a_ready, 1)
                for n in range(FT):
                    u = U_DN + n
                    if n >= 8 and n % 8 < 2:
                        norm_lo(l, 2, n // 8 * 2 - 2 + n % 2)
                    if n % 8 >= 6:
                        m = n // 8 * 2 + n % 2
                        unit_done(dve, l, u)
                        dve.tensor_tensor(x[:, m, :], main[(O_DN + m) % 4][:, 0:TOK], x[:, m, :], ALU.add)\
                           .then_inc(out_taken, 1)
                    if u + 3 < UNITS:
                        split_lo(l, u + 3)
                check_steps()
            dve.wait_ge(std_ready, DEPTH * 2 + 1)
            dve.reciprocal(rstd[:, :], std[:, :]).then_inc(lb_step, 1)
            dve.wait_ge(lb_step, 8)
            for k in range(KT):
                dve.scalar_tensor_tensor(x[:, k, :], x[:, k, :], cur[:, C_G1 + k:C_G1 + k + 1], rstd[:, :], ALU.mult,
                                         ALU.mult).then_inc(y_out, 1)

        @block.gpsimd
        def _(pool):
            def squares(step, norm, ready, previous):
                for k in range(KT):
                    ready(k)
                    if k == 0:
                        previous()
                        step(pool.tensor_tensor(sq_sum[:, :], x[:, k, :], x[:, k, :], ALU.mult))
                        continue
                    step(pool.tensor_tensor(sq[:, :], x[:, k, :], x[:, k, :], ALU.mult))
                    ins = pool.tensor_tensor(sq_sum[:, :], sq_sum[:, :], sq[:, :], ALU.add)
                    if k < KT - 1:
                        step(ins)
                ins.then_inc(sq_ready, 1)

            pool_start, _ = stepper(pool, pool_setup, 0, 0)
            squares(pool_start, 0, lambda k: pool.wait_ge(x_in[k // (KT // 2)], 16), lambda: None)
            pool.sem_inc(u_used, 4)
            with pool.Fori(0, DEPTH) as l:
                step, check_steps = stepper(pool, pool_step, l, POOL_STEPS)
                z_ready(pool, l, CT_CQ)
                wait_ends(pool)
                pool.memset(att[:, :, :, :].rearrange("p a b c -> p (a b c)"), 0.0).then_inc(att_clear, 1)
                pool.memset(q_heads[:, :, :, :].rearrange("p a b c -> p (a b c)"), 0.0)
                pool.memset(k_lv[:, :, :, :].rearrange("p a h t -> p (a h t)"), 0.0)
                step(pool.memset(suf_f[:, :, :].rearrange("p a b -> p (a b)"), 1.0))
                pool.wait_ge(decays, l + 1)
                z_ready(pool, l, CT_CQ + 1)
                for i, half in enumerate(LEVELS, 1):
                    if i >= 3:
                        take(pool, l, f"level {i - 2} 1")
                    def halves(t, s, half=half):
                        return t.rearrange("p h (n s t) -> p h n s t", s=2, t=half)[:, :, :, s, :]
                    for hp in range(2):
                        one = slice(hp, hp + 1)
                        pool.tensor_tensor(halves(q_lv[:, i % 2, one, :], 1),
                                           halves(z[:, CT_CQ + hp:CT_CQ + hp + 1, 0:PROMPT], 1),
                                           halves(cum_f[:, one, :], 1), ALU.mult)
                        ins = pool.tensor_tensor(halves(k_lv[:, i % 2, one, :], 0), halves(kg[:, one, 0:PROMPT], 0),
                                                 halves(suf_f[:, one, :], 0), ALU.mult)
                    step(ins)
                    pool.sem_inc(level_ready, 1)
                    suf = suf_f[:, :, :].rearrange("p h (n s t) -> p (h n) s t", s=2, t=half)
                    cum = cum_f[:, :, :].rearrange("p h (n s t) -> p (h n) s t", s=2, t=half)
                    n = PROMPT // half
                    step(pool.tensor_tensor(suf[:, :, 0, :], suf[:, :, 0, :],
                                            cum[:, :, 1, half - 1:half].to_broadcast([P, n, half]), ALU.mult))
                    if i < 8:
                        step(pool.tensor_tensor(cum[:, :, 1, :], cum[:, :, 1, :],
                                                cum[:, :, 0, half - 1:half].to_broadcast([P, n, half]), ALU.mult))
                take(pool, l, "level 7 1")
                pool.tensor_tensor(q_lv[:, 1, :, :], kg[:, :, 0:PROMPT], suf_f[:, :, :], ALU.mult).then_inc(final_keys, 1)
                pool.wait_ge(state_in, (l * 5 + 5) * 16)
                pool.wait_ge(outer_ready, l * 2 + 2)
                fs = f_s[:, :, :].rearrange("p h b -> p b h").unsqueeze(3).to_broadcast([P, SAMPLES, 2, HD])
                step(pool.tensor_tensor(state_s[:, :, :, :], state_s[:, :, :, :], fs, ALU.mult))
                pool.tensor_tensor(state_s[:, :, :, :], state_s[:, :, :, :], kv_outer, ALU.add)\
                    .then_inc(state_s_ready, 1)
                pool.wait_ge(sigmoids, 2 * l + 2)
                pool.tensor_tensor(z[:, CT_CO:CT_CO + 2, :], z[:, CT_CO:CT_CO + 2, :], o_c[:, :, :], ALU.mult)\
                    .then_inc(silu_ready, 1)
                for ct in range(6):
                    take(pool, l, f"rotate {ct}")
                    step(pool.tensor_tensor(z[:, ct, :], z[:, ct, :], cos, ALU.mult))
                    pool.wait_ge(sin_ready, l * 6 + ct + 1)
                    pool.tensor_tensor(z[:, ct, :], z[:, ct, :], rope_sin[:, ct, :], ALU.add).then_inc(roped, 1)
                pool.wait_ge(roped, l * 6 + 6)
                for h in range(2):
                    rows = slice(h * HD, (h + 1) * HD)
                    wait_ends(pool)
                    step(pool.tensor_copy(q_heads[rows, :, :, h], z[rows, CT_Q:CT_Q + NG, PROMPT:TOK]))
                pool.sem_inc(q_heads_ready, 1)
                pool.wait_ge(o_ready, 2 * l + 2)
                pool.tensor_tensor(z[:, CT_CF:CT_CF + 2, :], o_c[:, :, :], o_c[:, :, :], ALU.mult).then_inc(o_sq_ready, 1)
                z_ready(pool, l, CT_GC + 2)
                pool.wait_ge(stored, l * STORES * 16 + 16)
                pool.tensor_tensor(conv_in[:, :, 2:2 + PROMPT], z[:, CT_HB:CT_HB + 3, 0:PROMPT],
                                   z[:, CT_GC:CT_GC + 3, 0:PROMPT], ALU.mult)
                step(pool.tensor_tensor(conv_u[:, :, :], z[:, CT_HB:CT_HB + 3, PROMPT:TOK],
                                        z[:, CT_GC:CT_GC + 3, PROMPT:TOK], ALU.mult))
                pool.sem_inc(conv_in_ready, 1)
                pool.tensor_copy(conv_new[:, :, :, 0], conv_s[:, :, :, 1])
                pool.tensor_copy(conv_new[:, :, :, 1], conv_u[:, :, :]).then_inc(conv_new_ready, 1)
                pool.wait_ge(o_inv, l + 1)
                pool.tensor_tensor(o_c[:, :, :], o_c[:, :, :], z[:, CT_CI:CT_CI + 2, :], ALU.mult).then_inc(o_scaled, 1)
                pool.wait_ge(conv_out, l + 1)
                pool.tensor_tensor(z[:, CT_GB:CT_GB + 3, :], z[:, CT_GB:CT_GB + 3, :], z[:, CT_GC:CT_GC + 3, :],
                                   ALU.mult).then_inc(yb_ready, 1)
                for m in range(KT):
                    for j in range(3):
                        after_taken(pool, l, f"branch {m} {j}")
                    if m >= 2:
                        pool.wait_ge(mix_lo_ready, l * KT + m - 1)
                    s = m % 2
                    step(pool.tensor_tensor(gated[:, s, 0, :], gated[:, s, 0, :], gated[:, s, 1, :], ALU.add))
                    pool.tensor_tensor(mix[:, s, :], gated[:, s, 0, :], gated[:, s, 2, :], ALU.add).then_inc(mix_ready, 1)
                squares(step, 1, lambda m: x_ready(pool, l, 1, m), lambda: take(pool, l, "norm1"))
                squares(step, 2, lambda m: x_ready(pool, l, 2, m), lambda: take(pool, l, "norm2"))
                check_steps()


def constants():
    c = np.zeros((P, NCONST), np.float32)
    c[:, K_ID:K_ID + P] = np.eye(P)
    for head in range(2):
        for i in range(HD // 2):
            lo, hi = head * HD + i, head * HD + HD // 2 + i
            c[hi, K_ROT + lo] = -1.0
            c[lo, K_ROT + hi] = 1.0
    c[:, K_ONE:K_ONE + P] = 1.0
    for head in range(2):
        r = slice(head * HD, (head + 1) * HD)
        c[r, K_BLK + head * HD:K_BLK + (head + 1) * HD] = 1.0 / HD
    half = HD // 2
    inv = (np.float32(10000.0) ** (-np.arange(half, dtype=np.float32) / np.float32(half))).astype(np.float32)
    pos = np.concatenate([np.arange(PROMPT), np.full(SAMPLES, PAST)]).astype(np.float32)
    ang = inv[np.arange(P) % half][:, None] * pos[None, :]
    c[:, K_COS:K_COS + TOK] = np.cos(ang.astype(np.float32))
    c[:, K_SIN:K_SIN + TOK] = np.sin(ang.astype(np.float32))
    for b in range(SAMPLES):
        for h in range(2):
            for g in range(NG):
                c[b * 2 + h, K_DIAG + g * SAMPLES + b] = 1.0
            c[b * 2 + h, K_HSEL + h * HD:K_HSEL + (h + 1) * HD] = 1.0
    return c


def band_masks():
    out = []
    for q0, n in ((0, P), (P, PROMPT)):
        for win, dil in GROUPS:
            q = q0 + np.arange(P)[:, None]
            k = np.arange(n)[None, :]
            ok = (k <= q) & ((q - k) % dil == 0) & (q - k <= win)
            out.append(np.where(ok, 0.0, NEG))
    return np.concatenate(out, 1).astype(np.float32)


def level_masks():
    s, t = np.arange(P)[:, None], np.arange(P)[None, :]
    out = [s == t]
    for half in LEVELS[:-1]:
        late = (t[0] % (2 * half) >= half).nonzero()[0]
        out.append(((s // (2 * half) == t // (2 * half)) & (s % (2 * half) < half))[:, late])
    return np.concatenate(out, 1).astype(np.float32)


def kernel(x_prompt, x_sample, cache_kv_w128, cache_kv_w512, cache_kv_w2048, state_conv, state_hgrn,
           w_in, b_gate, norm1, conv_w, hgrn_lb, hgrn_norm, w_pa, w_pb, w_pc, w_o, norm2, w_up, w_down, norm_f):
    import concourse.bacc as bacc
    from concourse.bass_utils import run_bass_kernel_spmd

    A = np.ascontiguousarray

    def columns(a):
        a = np.asarray(a)
        return a.reshape(DEPTH, -1, P).transpose(2, 0, 1)

    cw = np.asarray(conv_w).reshape(DEPTH, 3 * 3 * P)
    arrays = {
        "consts": constants(),
        "bands": band_masks(),
        "levels": level_masks(),
        "gain0": A(columns(norm1)[:, 0]),
        "params": A(np.concatenate([columns(np.concatenate([np.asarray(norm1)[1:], np.asarray(norm_f)[None]])),
                                    columns(norm2), columns(b_gate), columns(cw),
                                    columns(hgrn_norm)], 2)),
        "hlb": A(columns(hgrn_lb)),
        "xT": A(np.concatenate([np.asarray(x_prompt)[0], np.asarray(x_sample)[:, 0]], 0).T),
        "w_in": A(w_in), "w_o": A(w_o), "w_up": A(w_up), "w_down": A(w_down),
        "w_br": A(np.concatenate([np.asarray(w_pa), np.asarray(w_pb), np.asarray(w_pc)], 1)),
        "state_convT": A(np.asarray(state_conv).reshape(DEPTH, SAMPLES, 2, 3, P).transpose(0, 4, 3, 1, 2)),
        "state_hgrn": A(state_hgrn),
    }
    for g, c in enumerate((cache_kv_w128, cache_kv_w512, cache_kv_w2048)):
        arrays[f"cache{g}"] = A(np.asarray(c).reshape(DEPTH, SAMPLES, -1, ROW))
    outs = {"yT": (D_MODEL, TOK), "convpT": (DEPTH, P, 3, 2), "convsT": (DEPTH, P, 3, SAMPLES, 2),
            "hgp": (DEPTH, 1, 4, HD, HD), "hgs": (DEPTH, SAMPLES, 4, HD, HD)}
    for g, (win, _) in enumerate(GROUPS):
        outs[f"kvp{g}"] = (DEPTH, 1, win, ROW)
        outs[f"kvs{g}"] = (DEPTH, SAMPLES, win, ROW)

    nc = bacc.Bacc("TRN2", target_bir_lowering=False, num_devices=1)
    io = {n: nc.dram_tensor(f"in_{n}", a.shape, mybir.dt.from_np(a.dtype), kind="ExternalInput").ap()
          for n, a in arrays.items()}
    io |= {n: nc.dram_tensor(f"out_{n}", s, F32, kind="ExternalOutput").ap() for n, s in outs.items()}
    trunk(nc, io)
    r = run_bass_kernel_spmd(nc, [{f"in_{n}": a for n, a in arrays.items()}], core_ids=[0]).results[0]
    r = {n: r[f"out_{n}"] for n in outs}

    y = r["yT"].T
    kvp = [r[f"kvp{g}"].reshape(DEPTH, 1, win, 2, 2, HD) for g, (win, _) in enumerate(GROUPS)]
    kvs = [r[f"kvs{g}"].reshape(DEPTH, SAMPLES, win, 2, 2, HD) for g, (win, _) in enumerate(GROUPS)]
    conv_p = r["convpT"].transpose(0, 3, 2, 1).reshape(DEPTH, 1, 2, 3 * P)
    conv_s = r["convsT"].transpose(0, 3, 4, 2, 1).reshape(DEPTH, SAMPLES, 2, 3 * P)
    return (A(y[None, :PROMPT]), A(y[PROMPT:, None]), *kvp, A(conv_p), r["hgp"], *kvs, A(conv_s), r["hgs"])
```

```python
from contextlib import ExitStack

import numpy as np

import concourse.bass as bass
from concourse import mybir

F32 = mybir.dt.float32
F32R = mybir.dt.float32r
U32 = mybir.dt.uint32
ALU = mybir.AluOpType
ACT = mybir.ActivationFunctionType
AX_X = mybir.AxisListType.X

P = 128
D_MODEL, DEPTH, PROMPT, SAMPLES, PAST = 1024, 2, 256, 8, 1024
TOK = PROMPT + SAMPLES
KT = D_MODEL // P
HD = 64
HALF = P // 2
GROUPS = ((128, 1), (512, 4), (2048, 16))
NG = len(GROUPS)
BAND = 128
D_FF = 4 * D_MODEL
FT = D_FF // P
EPS = 1e-6
LB_FLOOR = 1e-30
NEG = -1e30
SCALE = HD ** -0.5
ROW = 2 * 2 * HD

CT_Q, CT_K, CT_V, CT_HB, CT_GB, CT_GC, CT_CQ, CT_CF, CT_CI, CT_CO, CT_GATE = 0, 3, 6, 9, 12, 15, 18, 20, 22, 24, 26
N_GATE = 24
PAIR_ORDER = [10, 9, 11, 12, 0, 1, 2, 3, 4, 5, 6, 7, 8] + list(range(13, 25))
CT_OF_UNIT = [2 * c + h for c in PAIR_ORDER for h in range(2)]
UNIT_OF_CT = {ct: u for u, ct in enumerate(CT_OF_UNIT)}
BRANCHES, BRANCH_GATE = ((1, 3), (4, 2), (0, 1)), (1, 2, 0)
BT = 6

U_IN, U_BR, U_O, U_UP, U_DN, UNITS = 0, 50, 58, 66, 98, 130
O_IN, O_O, O_UP, O_DN, OUTS = 0, 50, 58, 90, 98
LAST_BANK = (O_DN + KT - 1) % 4
RING = 4
PAIRS = UNITS // 2
LEVELS = [1, 2, 4, 8, 16, 32, 64, 128]

TURNS = (
    ["norm1"]
    + ["values T", "sample values T"]
    + [f"level {i} {h}" for i in range(9) for h in range(2)]
    + ["sample values 0", "sample values 1"]
    + ["recurrence", "decayed keys T", "state"]
    + ["kv T 0", "kv T 1", "kv T 2", "sample recurrence"]
    + ["sample kv T 0", "sample kv T 1", "sample q T"]
    + ["head norm 0", "head norm 1"]
    + ["scores 0 0", "scores 0 1", "scores 0 2"]
    + ["probs T 0 0", "probs T 0 1", "probs T 0 2"]
    + ["scores 1 0", "scores 1 1", "scores 1 2"]
    + ["attend 0"]
    + ["probs T 1 0", "probs T 1 1", "probs T 1 2", "attend 1"]
    + ["sample scores T", "sample probs T", "sample attend"]
    + [f"branch {m} {j}" for m in range(KT) for j in range(3)]
    + ["norm2"]
)
TURN = {name: i for i, name in enumerate(TURNS)}
BANK_TURNS = [len(TURNS[b::4]) for b in range(4)]
OTHER_SIGNAL = {f"branch {m} 2" for m in range(KT)}
READY_TURNS = [sum(name not in OTHER_SIGNAL for name in TURNS[b::4]) for b in range(4)]
READY_INDEX = {name: sum(t not in OTHER_SIGNAL for t in TURNS[i % 4:i + 1:4]) for name, i in TURN.items()}

DVE_STEPS, ACT_STEPS, POOL_STEPS = 31, 3, 64

C_G1, C_G2, C_BG, C_CW, C_HN, C_LB, C_OM, NPAR = 0, 8, 16, 40, 49, 51, 53, 55
K_ID, K_ONE, K_BLK, K_COS, K_SIN, K_DIAG, K_HSEL = 0, 128, 256, 384, 648, 912, 936
NCONST = 936 + 128


def ring_before(i, n):
    return (3, 4, 1, 2)[i] if i < 4 else i + 1


def trunk(nc, io):
    with ExitStack() as ctx:
        def sb(name, shape, dt=F32, stack=ctx):
            return stack.enter_context(nc.sbuf_tensor(name, shape, dt))

        def sem(name):
            return ctx.enter_context(nc.semaphore(name))

        raw = sb("raw", [P, 2, KT, 2 * P])
        w_hi = sb("w_hi", [P, RING, KT, P], F32R)
        w_lo = sb("w_lo", [P, RING, KT, P], F32R)
        x = sb("x", [P, KT, TOK])
        h_hi = sb("h_hi", [P, KT, TOK], F32R)
        h_lo = sb("h_lo", [P, KT, TOK], F32R)
        consts = sb("consts", [P, NCONST])
        bands = sb("bands", [P, 9 * P])
        levels = sb("levels", [P, P + 7 * HALF])
        par = sb("par", [P, DEPTH, NPAR])
        cur = sb("cur", [P, NPAR])
        hlb = sb("hlb", [P, DEPTH, 2])
        lb_tmp = sb("lb_tmp", [P, 8, 2])
        eps = sb("eps", [P, 1])
        std = sb("std", [P, TOK])
        rstd = sb("rstd", [P, TOK])
        sq = sb("sq", [P, TOK])
        sq_sum = sb("sq_sum", [P, TOK])
        zeros = sb("zeros", [P, 512])
        conv_in = sb("conv_in", [P, 3, 2 + PROMPT])

        with ExitStack() as early:
            gates = sb("gates", [P, N_GATE, TOK], stack=early)
            z = sb("z", [P, CT_GATE, TOK], stack=early)
            kv_tm = sb("kv_tm", [P, 2, NG, 2, P], stack=early)
            kv_s = sb("kv_s", [SAMPLES, NG, 2, P], stack=early)
            q_s = sb("q_s", [SAMPLES, NG, P], stack=early)
            kg = sb("kg", [P, 2, TOK], stack=early)
            v_tm = sb("v_tm", [P, 2, 2, P], stack=early)
            v_s = sb("v_s", [SAMPLES, 2, P], stack=early)
            o_c = sb("o_c", [P, 2, TOK], stack=early)
            y_a = sb("y_a", [P, TOK], stack=early)
            f_s = sb("f_s", [P, 2, SAMPLES], stack=early)
            state_p = sb("state_p", [P, 2, HD], stack=early)
            conv_s = sb("conv_s", [P, 3, SAMPLES, 2], stack=early)
            conv_u = sb("conv_u", [P, 3, SAMPLES], stack=early)
            conv_new = sb("conv_new", [P, 3, SAMPLES, 2], stack=early)
            q_heads = sb("q_heads", [P, NG, SAMPLES, 2], stack=early)
            sc = sb("sc", [P, NG, SAMPLES, 2], stack=early)
            pr_s = sb("pr_s", [P, NG, SAMPLES, 2], stack=early)
            s_rows = sb("s_rows", [2 * SAMPLES, NG * P + NG], stack=early)
            new_sc = sb("new_sc", [2 * SAMPLES, NG, SAMPLES], stack=early)
            s_stat = sb("s_stat", [2 * SAMPLES, 3], stack=early)
            new_pv = sb("new_pv", [P, NG, SAMPLES], stack=early)
            ya_new = sb("ya_new", [P, SAMPLES], stack=early)
            stat = sb("stat", [P, 2, 4], stack=early)
            with ExitStack() as s:
                cum_f = sb("cum_f", [P, 2, PROMPT], stack=s)
                suf_f = sb("suf_f", [P, 2, PROMPT], stack=s)
                q_lv = sb("q_lv", [P, 2, 2, PROMPT], stack=s)
                k_lv = sb("k_lv", [P, 2, 2, PROMPT], stack=s)
                att = sb("att", [P, 2, 4, P], stack=s)
                att_far = sb("att_far", [P, 2, 2, P], stack=s)
                k_tm = sb("k_tm", [P, 2, 2, P], stack=s)
                state_s = sb("state_s", [P, SAMPLES, 2, HD], stack=s)
            with ExitStack() as s:
                v_cache = sb("v_cache", [P, SAMPLES, NG, P], stack=s)
                probs = sb("probs", [P, 9 * P], stack=s)
                probs_t = sb("probs_t", [P, 9, P], stack=s)
            sb("shared_region", [P, 48 * P], stack=early)
            with ExitStack() as s:
                k_cache = sb("k_cache", [P, SAMPLES, NG, P], stack=s)
            y_hi = sb("y_hi", [P, BT, TOK], F32R, stack=early)
            y_lo = sb("y_lo", [P, BT, TOK], F32R, stack=early)
        with ExitStack() as s:
            sb("gates_below", [P, N_GATE, TOK], stack=s)
            mix_hi = sb("mix_hi", [P, KT, TOK], F32R, stack=s)
            mix_lo = sb("mix_lo", [P, KT, TOK], F32R, stack=s)
            gated = sb("gated", [P, 2, 3, TOK], stack=s)
            mix = sb("mix", [P, 2, TOK], stack=s)
        a_hi = sb("a_hi", [P, FT, TOK], F32R)
        a_lo = sb("a_lo", [P, FT, TOK], F32R)
        u_relu = sb("u_relu", [P, RING, TOK])
        a_full = sb("a_full", [P, RING, TOK])
        kv_outer = gates[:, 0:4, :].rearrange("p a t -> p (a t)")[:, 0:SAMPLES * 2 * HD].rearrange(
            "p (b h v) -> p b h v", b=SAMPLES, h=2)
        swapped_qk = gates[:, 4:10, :]
        q_rows = gates[:, 12:24, :].rearrange("p a t -> p (a t)")[:, 0:SAMPLES * NG * P].rearrange(
            "p (b g c) -> p b g c", b=SAMPLES, g=NG)

        ident = consts[:, K_ID:K_ID + P]
        ones = consts[:, K_ONE:K_ONE + P]
        blk = consts[:, K_BLK:K_BLK + P]
        cos = consts[:, K_COS:K_COS + TOK]
        sin = consts[:, K_SIN:K_SIN + TOK]
        diag = consts[0:16, K_DIAG:K_DIAG + 24]
        hsel = consts[0:16, K_HSEL:K_HSEL + P]

        main = [ctx.enter_context(nc.psum_tensor(f"main{i}", [P, 512], F32)) for i in range(4)]
        small = [ctx.enter_context(nc.psum_tensor(f"small{i}", [P, 512], F32)) for i in range(4)]

        gain_in, x_in = sem("gain_in"), [sem("x_in0"), sem("x_in1")]
        params_in, hlb_in, consts_in = sem("params_in"), sem("hlb_in"), sem("consts_in")
        levels_in, bands_in = sem("levels_in"), sem("bands_in")
        first_landed = sem("first_landed")
        raw_landed = [sem("raw_landed0"), sem("raw_landed1")]
        w_hi_ready = sem("w_hi_ready")
        w_lo_ready = sem("w_lo_ready")
        w_used = sem("w_used")
        out_taken = sem("out_taken")
        bank_ready = [sem(f"bank_ready{b}") for b in range(4)]
        bank_taken = [sem(f"bank_taken{b}") for b in range(4)]
        dve_step, act_step, pool_step = sem("dve_step"), sem("act_step"), sem("pool_step")
        pool_setup = sem("pool_setup")
        layer_params = sem("layer_params")
        h_hi_ready = sem("h_hi_ready")
        h_ready = sem("h_ready")
        sq_ready = sem("sq_ready")
        std_ready = sem("std_ready")
        setup_done, bank_cleared = sem("setup_done"), sem("bank_cleared")
        lb_ready, lb_exp, lb_step = sem("lb_ready"), sem("lb_exp"), sem("lb_step")
        sigmoids = sem("sigmoids")
        decays = sem("decays")
        kg_ready = sem("kg_ready")
        att_clear = sem("att_clear")
        v_tm_ready = sem("v_tm_ready")
        v_s_ready = sem("v_s_ready")
        level_ready = sem("level_ready")
        masked = sem("masked")
        far_ready = sem("far_ready")
        outer_ready = sem("outer_ready")
        state_s_ready = sem("state_s_ready")
        state_s_used = sem("state_s_used")
        state_in = sem("state_in")
        final_keys = sem("final_keys")
        k_tm_ready = sem("k_tm_ready")
        state_p_ready = sem("state_p_ready")
        o_ready = sem("o_ready")
        o_sq_ready = sem("o_sq_ready")
        o_std = sem("o_std")
        silu_ready = sem("silu_ready")
        o_scaled = sem("o_scaled")
        o_inv = sem("o_inv")
        yc_ready = sem("yc_ready")
        halves_swapped = sem("halves_swapped")
        sin_ready = sem("sin_ready")
        q_out, q_rows_in = sem("q_out"), [sem("q_rows_in0"), sem("q_rows_in1")]
        roped = sem("roped")
        conv_in_ready = sem("conv_in_ready")
        conv_out = sem("conv_out")
        yb_ready = sem("yb_ready")
        conv_new_ready = sem("conv_new_ready")
        kv_tm_ready = sem("kv_tm_ready")
        kv_s_ready = sem("kv_s_ready")
        q_s_ready = sem("q_s_ready")
        q_heads_ready = sem("q_heads_ready")
        keys_in, values_in = sem("keys_in"), sem("values_in")
        maxed = sem("maxed")
        exped = sem("exped")
        probs_ready = sem("probs_ready")
        probs_t_ready = sem("probs_t_ready")
        s_scored, s_rows_ready, s_exped = sem("s_scored"), sem("s_rows_ready"), sem("s_exped")
        s_probs, s_probs_t = sem("s_probs"), sem("s_probs_t")
        ya_ready = sem("ya_ready")
        y_hi_ready, y_ready = sem("y_hi_ready"), sem("y_ready")
        gates_ready = sem("gates_ready")
        mix_ready, mix_hi_ready, mix_lo_ready = sem("mix_ready"), sem("mix_hi_ready"), sem("mix_lo_ready")
        u_used = sem("u_used")
        a_hi_ready, a_ready = sem("a_hi_ready"), sem("a_ready")
        states_stored = sem("states_stored")
        stored = sem("stored")
        shifted = sem("shifted")
        y_out = sem("y_out")

        waits_over = sem("waits_over")

        def use_bank(pe, l, name):
            i = TURN[name]
            pe.wait_ge(bank_taken[i % 4], l * BANK_TURNS[i % 4] + i // 4 + 1)
            return small[i % 4]

        def done(ins, name):
            ins.then_inc(bank_ready[TURN[name] % 4], 1)

        def take(eng, l, name):
            b = TURN[name] % 4
            eng.wait_ge(bank_ready[b], l * READY_TURNS[b] + READY_INDEX[name])
            return small[b]

        def taken(ins, name):
            ins.then_inc(bank_taken[TURN[name] % 4], 1)

        def after_taken(eng, l, name):
            i = TURN[name]
            eng.wait_ge(bank_taken[i % 4], l * BANK_TURNS[i % 4] + i // 4 + 2)

        def wait_ends(eng):
            eng.sem_inc(waits_over, 1)

        def unit_done(eng, l, u):
            eng.wait_ge(w_used, l * UNITS + 4 + u + 1)

        def z_ready(eng, l, ct):
            eng.wait_ge(out_taken, l * OUTS + 4 + UNIT_OF_CT[ct] + 1)

        def x_ready(eng, l, n, m=KT - 1):
            eng.wait_ge(out_taken, l * OUTS + 4 + (0, O_O + m + 1, O_DN + m + 1)[n])

        def stepper(eng, semaphore, l, total):
            count = [0]

            def step(ins):
                count[0] += 1
                ins.then_inc(semaphore, 1)
                eng.wait_ge(semaphore, l * total + count[0])

            def check():
                assert count[0] == total, (semaphore, count[0])
            return step, check

        def raw_of(u, k=KT):
            return raw[:, (u // 2) % 2, 0:k, (u % 2) * P:(u % 2) * P + P]

        STORES, STATE_STORES = 10, 6
        SHIFTS = 56

        block = ctx.enter_context(nc.Block())

        @block.sync
        def _(sp):
            sp.dma_start(cur[:, C_G1:C_G1 + KT], io["gain0"]).then_inc(gain_in, 16)
            sp.dma_start(hlb[:, :, :], io["hlb"]).then_inc(hlb_in, 16)
            for i in range(2):
                ks = slice(i * KT // 2, (i + 1) * KT // 2)
                sp.dma_start(x[:, ks, :], io["xT"].rearrange("(k p) t -> p k t", p=P)[:, ks, :]).then_inc(x_in[i], 16)
            sp.dma_start(par[:, :, 0:C_LB], io["params"]).then_inc(params_in, 16)

            def weights(l, p, src, first, k=KT):
                sp.wait_ge(w_lo_ready, first)
                wait_ends(sp)
                if p == 0:
                    sp.dma_start(raw[:, 0, :, 0:P], src[:, :, 0:P]).then_inc(first_landed, 16)
                    sp.dma_start(raw[:, 0, :, P:2 * P], src[:, :, P:2 * P]).then_inc(raw_landed[0], 16)
                    return
                sp.dma_start(raw[:, p % 2, 0:k, :], src).then_inc(raw_landed[p % 2], 16)

            def w_in_pair(l, col):
                return io["w_in"][bass.ds(l, 1), :, bass.ds(col, 2 * P)].rearrange("a (k p) n -> p (a k) n", p=P)

            def before(l, p):
                return l * UNITS + ((4, 2)[p] if p < 2 else 2 * p + 2)

            def store(dst, src, signal=stored):
                sp.dma_start(dst, src).then_inc(signal, 16)

            def shift(l, g, b, first, rows):
                win = GROUPS[g][0]
                n = 16 if rows % 16 == 0 else rows
                src = io[f"cache{g}"][bass.ds(l, 1), bass.ds(b, 1), first + 1:first + 1 + rows]
                dst = io[f"kvs{g}"][bass.ds(l, 1), bass.ds(b, 1), first:first + rows]
                assert first + rows <= win - 1
                sp.dma_start(dst.rearrange("l b (n r) c -> (l b n) (r c)", n=n),
                             src.rearrange("l b (n r) c -> (l b n) (r c)", n=n)).then_inc(shifted, 16)

            sp.sem_inc(stored, 16)
            sp.sem_inc(states_stored, 16)
            sp.wait_ge(setup_done, 1)
            with sp.Fori(0, DEPTH) as l:
                for p in range(25):
                    weights(l, p, w_in_pair(l, PAIR_ORDER[p] * 2 * P), before(l, p))
                    if p == 2:
                        unit_done(sp, l, 0)
                        sp.wait_ge(states_stored, l * STATE_STORES * 16 + 16)
                        hg = io["state_hgrn"][bass.ds(l, 1)].rearrange("l b (hp h) c v -> h hp c (l b) v", h=2)
                        for h in range(2):
                            for hp in range(2):
                                sp.dma_start(state_s[h * HD:(h + 1) * HD, :, hp, :], hg[h, hp]).then_inc(state_in, 16)
                        sp.dma_start(conv_s[:, :, :, :], io["state_convT"][bass.ds(l, 1)].rearrange(
                            "l p j b s -> (l p) j b s")).then_inc(state_in, 16)
                    if p == 10:
                        z_ready(sp, l, CT_V - 1)
                        for i in range(4):
                            own, other = (slice(n * HD // 2, (n + 1) * HD // 2) for n in (i, i ^ 1))
                            sp.dma_start(swapped_qk[own, :, :], z[other, CT_Q:CT_V, :]).then_inc(halves_swapped, 16)
                    if p == 4:
                        for g, (win, dil) in enumerate(GROUPS):
                            n = min(BAND, PAST // dil)
                            rows = io[f"cache{g}"][bass.ds(l, 1)].rearrange("l b (n d) c -> n (l b) d c", d=dil)
                            sp.dma_start(k_cache[0:n, :, g, :], rows[BAND - n:BAND, :, 0, 0:P]).then_inc(keys_in, 16)
                    if 5 <= p < 13:
                        shift(l, 1, p - 5, 0, 496)
                    if p in (9, 11, 13, 24):
                        shift(l, 2, 2 * (9, 11, 13, 24).index(p) + 1, 1024, 512)
                    if p == 14:
                        sp.wait_ge(state_p_ready, l + 1)
                        wait_ends(sp)
                        hg = io["hgp"][bass.ds(l, 1)].rearrange("l b (hp h) c v -> h c (l b hp) v", h=2)
                        for h in range(2):
                            store(hg[h], state_p[h * HD:(h + 1) * HD, :, :], states_stored)
                    if p == 14:
                        sp.wait_ge(state_s_used, l + 1)
                        hg = io["hgs"][bass.ds(l, 1)].rearrange("l b (hp h) c v -> h hp c (l b) v", h=2)
                        for h in range(2):
                            for hp in range(2):
                                store(hg[h, hp], state_s[h * HD:(h + 1) * HD, :, hp, :], states_stored)
                    if p == 15:
                        sp.wait_ge(kv_tm_ready, l * NG + NG)
                        wait_ends(sp)
                        for g, (win, dil) in enumerate(GROUPS):
                            for tb in range(2) if win > BAND else (1,):
                                r = max(win, PROMPT) - PROMPT + tb * P - (PROMPT - win if win < PROMPT else 0)
                                store(io[f"kvp{g}"][bass.ds(l, 1), 0, r:r + P].rearrange("l r c -> (l r) c"),
                                      kv_tm[:, tb, g, :, :].rearrange("p a c -> p (a c)"))
                        sp.wait_ge(kv_s_ready, l * 2 + 2)
                        for g, (win, dil) in enumerate(GROUPS):
                            store(io[f"kvs{g}"][bass.ds(l, 1), :, win - 1].rearrange("l b c -> (l b) c"),
                                  kv_s[:, g, :, :].rearrange("p a c -> p (a c)"))
                        sp.wait_ge(q_s_ready, l + 1)
                        sp.dma_start(io["q_scratch"], q_s[:, :, :].rearrange("p g c -> p (g c)")).then_inc(q_out, 16)
                    if p in (16, 17):
                        sp.wait_ge(q_out, l * 16 + 16)
                        bs = slice((p - 16) * SAMPLES // 2, (p - 15) * SAMPLES // 2)
                        sp.dma_start(q_rows[:, bs, :, :].rearrange("p b g c -> p (b g c)"),
                                     io["q_scratch"][bs].rearrange("b c -> (b c)").unsqueeze(0).to_broadcast(
                                         [P, SAMPLES // 2 * NG * P])).then_inc(q_rows_in[p - 16], 16)
                    if 18 <= p < 18 + NG:
                        sp.wait_ge(o_ready, 2 * l + 2)
                        wait_ends(sp)
                        sp.wait_ge(state_p_ready, l + 1)
                        wait_ends(sp)
                        sp.wait_ge(states_stored, l * STATE_STORES * 16 + 16 + STATE_STORES * 16)
                        g, dil = p - 18, GROUPS[p - 18][1]
                        n = min(BAND, PAST // dil)
                        rows = io[f"cache{g}"][bass.ds(l, 1)].rearrange("l b (n d) c -> n (l b) d c", d=dil)
                        sp.dma_start(v_cache[0:n, :, g, :], rows[BAND - n:BAND, :, 0, P:2 * P]).then_inc(
                            values_in, 16)
                    if p == 17:
                        sp.wait_ge(conv_new_ready, l + 1)
                        store(io["convsT"][bass.ds(l, 1)].rearrange("l p j b s -> (l p) (j b s)"),
                              conv_new[:, :, :, :].rearrange("p j b s -> p (j b s)"))
                        store(io["convpT"][bass.ds(l, 1)].rearrange("l p j s -> (l p) j s"),
                              conv_in[:, :, PROMPT:PROMPT + 2])
                    if 20 <= p < 24:
                        for g, (win, dil) in enumerate(GROUPS):
                            n = (win - PROMPT) * ROW // (P * 512)
                            part = range(n)[(p - 20) * 2:(p - 20) * 2 + 2] if win > PROMPT else ()
                            if part:
                                sp.dma_start(
                                    io[f"kvp{g}"][bass.ds(l, 1), 0, 0:win - PROMPT].rearrange(
                                        "l (p r) c -> (l p) (r c)", p=P).rearrange("p (n c) -> p n c", n=n)[
                                            :, part.start:part.stop, :],
                                    zeros[:, :].unsqueeze(1).to_broadcast([P, len(part), 512])).then_inc(shifted, 16)
                    if p == 19:
                        for g, first in ((0, 112), (1, 496), (2, 2032)):
                            sp.dma_start(
                                io[f"kvs{g}"][bass.ds(l, 1), :, first:first + 15].rearrange("l b r c -> (l b) (r c)"),
                                io[f"cache{g}"][bass.ds(l, 1), :, first + 1:first + 16].rearrange(
                                    "l b r c -> (l b) (r c)")).then_inc(shifted, 16)
                    if 20 <= p < 24:
                        shift(l, 0, 2 * (p - 20), 0, 112)
                        shift(l, 0, 2 * (p - 20) + 1, 0, 112)
                for i in range(4):
                    p = U_BR // 2 + i
                    weights(l, p, io["w_br"][bass.ds(l, 1), :, i * 2 * P:(i + 1) * 2 * P].rearrange(
                        "a (k p) n -> p (a k) n", p=P), before(l, p), k=BT)
                    shift(l, 2, i, 1536, 496)
                for i in range(4):
                    p = U_O // 2 + i
                    weights(l, p, io["w_o"][bass.ds(l, 1), :, i * 2 * P:(i + 1) * 2 * P].rearrange(
                        "a (k p) n -> p (a k) n", p=P), before(l, p))
                    shift(l, 2, 4 + i, 1536, 496)
                with sp.Fori(0, FT // 4) as i:
                    for j in range(2):
                        p = U_UP // 2 + j
                        weights(l, p, io["w_up"][bass.ds(l, 1), :, bass.ds(i * 512 + j * 2 * P, 2 * P)].rearrange(
                            "a (k p) n -> p (a k) n", p=P), l * UNITS + i * 4 + 2 * p + 2)
                    shift(l, 2, i, 0, 512)
                with sp.Fori(0, 4) as i:
                    for kc in range(4):
                        p = U_DN // 2 + kc
                        weights(l, p, io["w_down"][bass.ds(l, 1), kc * D_MODEL:(kc + 1) * D_MODEL,
                                                   bass.ds(i * 2 * P, 2 * P)].rearrange(
                            "a (k p) n -> p (a k) n", p=P), l * UNITS + i * 8 + 2 * p + 2)
                        if kc < 3:
                            shift(l, 2, i * 2 + kc % 2, 512 + kc // 2 * 512, 512)
            for i in range(4):
                ks = slice(i * KT // 4, (i + 1) * KT // 4)
                sp.wait_ge(y_out, ks.stop)
                store(io["yT"].rearrange("(k p) t -> p k t", p=P)[:, ks, :], x[:, ks, :])
            sp.wait_ge(stored, 16 + DEPTH * STORES * 16 + 4 * 16)
            sp.wait_ge(states_stored, 16 + DEPTH * STATE_STORES * 16)
            sp.wait_ge(shifted, DEPTH * SHIFTS * 16)

        @block.tensor
        def _(pe):
            def unit(slot, out, rhs_hi, rhs_lo, k0, nk, wk0=0, start=True, stop=True, per_k=None):
                for k in range(nk):
                    if per_k is not None:
                        per_k(k)
                    wh, wl = w_hi[:, slot, wk0 + k, :], w_lo[:, slot, wk0 + k, :]
                    rh, rl = rhs_hi[:, k0 + k, :], rhs_lo[:, k0 + k, :]
                    pe.matmul(out[:, 0:TOK], wh, rh, start=start and k == 0, stop=False)
                    pe.matmul(out[:, 0:TOK], wh, rl, start=False, stop=False)
                    last = pe.matmul(out[:, 0:TOK], wl, rh, start=False, stop=stop and k == nk - 1)
                return last

            def sum_squares(l, name, n):
                pe.wait_ge(sq_ready, l * 2 + n + 1)
                bank = use_bank(pe, l, name)
                done(pe.matmul(bank[:, 0:TOK], ones, sq_sum[:, :], start=True, stop=True), name)

            def transposes(l, name, parts):
                bank = use_bank(pe, l, name)
                for col, src in parts:
                    k, n = src.shape[0], src.size() // src.shape[0]
                    mm = pe.transpose(bank[0:n, col:col + k], src, ident[0:k, 0:k])
                done(mm, name)

            def level(l, i):
                if i:
                    pe.wait_ge(level_ready, l * 8 + i)
                else:
                    pe.wait_ge(kg_ready, l + 1)
                    z_ready(pe, l, CT_CQ + 1)

                def operands(hp, h):
                    rows = slice(h * HD, (h + 1) * HD)
                    if i:
                        return k_lv[rows, i % 2, hp, :], q_lv[rows, i % 2, hp, :]
                    return kg[rows, hp, 0:PROMPT], z[rows, CT_CQ + hp, 0:PROMPT]

                def queries(qq, tb):
                    if not i:
                        return qq[:, tb * P:tb * P + P]
                    return qq[:, tb * P:tb * P + P].rearrange("p (n s t) -> p n s t", s=2, t=LEVELS[i - 1])[:, :, 1, :]
                w = HALF if i else P
                for h in range(2):
                    bank = use_bank(pe, l, f"level {i} {h}")
                    for hp in range(2):
                        kk, qq = operands(hp, h)
                        if i == 8:
                            c = hp * P
                            mm = pe.matmul(bank[:, c:c + P], kk[:, 0:P], qq[:, P:2 * P], start=True, stop=True)
                            continue
                        for tb in range(2):
                            c = (hp * 2 + tb) * w
                            mm = pe.matmul(bank[:, c:c + w], kk[:, tb * P:tb * P + P], queries(qq, tb),
                                           start=True, stop=True)
                    done(mm, f"level {i} {h}")

            def scores(l, h):
                rows = slice(h * HD, (h + 1) * HD)
                bank = use_bank(pe, l, f"scores {h} 0")
                for g in range(NG):
                    mm = pe.matmul(bank[:, g * P:g * P + P], z[rows, CT_Q + g, 0:P], z[rows, CT_K + g, 0:P],
                                   start=True, stop=True)
                done(mm, f"scores {h} 0")
                for j, gs in ((1, (0, 1)), (2, (2,))):
                    bank = use_bank(pe, l, f"scores {h} {j}")
                    for n, g in enumerate(gs):
                        mm = pe.matmul(bank[:, n * PROMPT:(n + 1) * PROMPT], z[rows, CT_Q + g, P:2 * P],
                                       z[rows, CT_K + g, 0:PROMPT], start=True, stop=True)
                    done(mm, f"scores {h} {j}")

            def attend(l, h):
                pe.wait_ge(probs_t_ready, l * 6 + h * 3 + 3)
                name = f"attend {h}"
                bank = use_bank(pe, l, name)
                rows = slice(h * HD, (h + 1) * HD)
                for g in range(NG):
                    pe.matmul(bank[rows, 0:P], kv_tm[:, 0, g, 1, rows], probs_t[:, g, :], start=g == 0, stop=g == NG - 1)
                for g in range(NG):
                    for tb in range(2):
                        mm = pe.matmul(bank[rows, P:2 * P], kv_tm[:, tb, g, 1, rows], probs_t[:, NG + 2 * g + tb, :],
                                       start=g == 0 and tb == 0, stop=g == NG - 1 and tb == 1)
                done(mm, name)

            def between(l, u):
                if u == 0:
                    pe.wait_ge(consts_in, 16)
                    sum_squares(l, "norm1", 0)
                if u == 6:
                    z_ready(pe, l, CT_CI + 1)
                    transposes(l, "values T", [((tb * 2 + hp) * P, z[:, CT_CI + hp, tb * P:tb * P + P])
                                               for tb in range(2) for hp in range(2)])
                    transposes(l, "sample values T", [(hp * P, z[:, CT_CI + hp, PROMPT:TOK]) for hp in range(2)])
                if 7 <= u < 16:
                    level(l, u - 7)
                if u == 16:
                    pe.wait_ge(v_s_ready, l + 1)
                    for i4 in range(2):
                        name = f"sample values {i4}"
                        bank = use_bank(pe, l, name)
                        for bb in range(4):
                            for h in range(2):
                                rows = slice(h * HD, (h + 1) * HD)
                                b = i4 * 4 + bb
                                mm = pe.matmul(bank[rows, bb * P:bb * P + P],
                                               ident[0:SAMPLES, b:b + 1].to_broadcast([SAMPLES, HD]),
                                               v_s[:, :, rows], start=True, stop=True)
                        done(mm, name)
                if u == 17:
                    pe.wait_ge(masked, l * 16 + 16)
                    pe.wait_ge(far_ready, 2 * l + 2)
                    pe.wait_ge(v_tm_ready, l + 1)
                    bank = use_bank(pe, l, "recurrence")
                    for hp in range(2):
                        for h in range(2):
                            rows = slice(h * HD, (h + 1) * HD)
                            c = hp * PROMPT
                            pe.matmul(bank[rows, c:c + P], v_tm[:, 0, hp, rows], att[:, h, hp * 2, :],
                                      start=True, stop=True)
                            pe.matmul(bank[rows, c + P:c + 2 * P], v_tm[:, 0, hp, rows], att_far[:, h, hp, :],
                                      start=True, stop=False)
                            mm = pe.matmul(bank[rows, c + P:c + 2 * P], v_tm[:, 1, hp, rows], att[:, h, hp * 2 + 1, :],
                                           start=False, stop=True)
                    done(mm, "recurrence")
                    pe.wait_ge(final_keys, l + 1)
                    transposes(l, "decayed keys T", [((tb * 2 + hp) * P, q_lv[:, 1, hp, tb * P:tb * P + P])
                                                     for tb in range(2) for hp in range(2)])
                if u == 18:
                    pe.wait_ge(k_tm_ready, l + 1)
                    bank = use_bank(pe, l, "state")
                    for hp in range(2):
                        for h in range(2):
                            rows = slice(h * HD, (h + 1) * HD)
                            for tb in range(2):
                                mm = pe.matmul(bank[rows, hp * HD:(hp + 1) * HD], k_tm[:, tb, hp, rows],
                                               v_tm[:, tb, hp, rows], start=tb == 0, stop=tb == 1)
                    done(mm, "state")
                for at, g in ((20, 0), (20, 1), (21, 2)):
                    if u == at:
                        pe.wait_ge(roped, l + 1)
                        transposes(l, f"kv T {g}", [((tb * 2 + kv) * P, z[:, (CT_K, CT_V)[kv] + g, tb * P:tb * P + P])
                                                    for tb in range(2) for kv in range(2)])
                if u in (21, 22):
                    hp = u - 21
                    if hp == 0:
                        pe.wait_ge(state_s_ready, l + 1)
                        bank = use_bank(pe, l, "sample recurrence")
                        wait_ends(pe)
                    else:
                        bank = small[TURN["sample recurrence"] % 4]
                    for b in range(SAMPLES):
                        for h in range(2):
                            rows = slice(h * HD, (h + 1) * HD)
                            mm = pe.matmul(bank[rows, hp * SAMPLES + b:hp * SAMPLES + b + 1],
                                           state_s[rows, b, hp, :], z[rows, CT_CQ + hp, PROMPT + b:PROMPT + b + 1],
                                           start=True, stop=True)
                    if hp == 1:
                        done(mm, "sample recurrence")
                if u == 22:
                    kvs = [z[:, (CT_K, CT_V)[kv] + g, PROMPT:TOK] for g in range(NG) for kv in range(2)]
                    transposes(l, "sample kv T 0", [(i * P, s) for i, s in enumerate(kvs[0:4])])
                    transposes(l, "sample kv T 1", [(i * P, s) for i, s in enumerate(kvs[4:6])])
                if u == 23:
                    transposes(l, "sample q T", [(g * P, z[:, CT_Q + g, PROMPT:TOK]) for g in range(NG)])
                if u == 24:
                    pe.wait_ge(o_sq_ready, l + 1)
                    for hp in range(2):
                        bank = use_bank(pe, l, f"head norm {hp}")
                        done(pe.matmul(bank[:, 0:TOK], blk, z[:, CT_CF + hp, :], start=True, stop=True),
                             f"head norm {hp}")
                if u in (25, 32):
                    scores(l, (u - 25) // 7)
                for h in range(2):
                    if u == 30 + 7 * h:
                        pe.wait_ge(probs_ready, l * 2 + h + 1)
                        for j in range(3):
                            transposes(l, f"probs T {h} {j}", [((b % 4) * P, probs[:, b * P:b * P + P])
                                                              for b in range(4 * j, min(4 * j + 4, 9))])
                    if u == 32 + 7 * h:
                        pe.wait_ge(kv_tm_ready, l * NG + NG)
                        attend(l, h)
                if u == 41:
                    pe.wait_ge(s_scored, l + 1)
                    pe.wait_ge(q_heads_ready, l + 1)
                    name = "sample scores T"
                    bank = use_bank(pe, l, name)
                    for g in range(NG):
                        pe.transpose(bank[0:16, g * P:g * P + P], sc[:, g, :, :].rearrange("p b h -> p (b h)"), ident)
                    for g in range(NG):
                        c = NG * P + g * SAMPLES
                        mm = pe.matmul(bank[0:16, c:c + SAMPLES], q_heads[:, g, :, :].rearrange("p b h -> p (b h)"),
                                       z[:, CT_K + g, PROMPT:TOK], start=True, stop=True)
                    done(mm, name)
                if u == 44:
                    pe.wait_ge(s_probs, l + 1)
                    name = "sample probs T"
                    bank = use_bank(pe, l, name)
                    for g in range(NG):
                        wait_ends(pe)
                        pe.transpose(bank[:, g * 16:g * 16 + 16], s_rows[:, g * P:g * P + P], ident[0:16, 0:16])
                    done(pe.matmul(bank[:, 64:64 + NG * SAMPLES], hsel, new_sc[:, :, :].rearrange("p g b -> p (g b)"),
                                   start=True, stop=True), name)
                if 46 <= u < 50:
                    name = "sample attend"
                    if u == 46:
                        pe.wait_ge(s_probs_t, l + 1)
                        pe.wait_ge(values_in, l * NG * 16 + NG * 16)
                        bank = use_bank(pe, l, name)
                    else:
                        bank = small[TURN[name] % 4]
                    for b in range((u - 46) * SAMPLES // 4, (u - 45) * SAMPLES // 4):
                        for g, (win, dil) in enumerate(GROUPS):
                            n = min(BAND, PAST // dil)
                            mm = pe.matmul(bank[:, 2 * b:2 * b + 2], v_cache[0:n, b, g, :], pr_s[0:n, g, b, :],
                                           start=g == 0, stop=g == NG - 1)
                    if u == 49:
                        done(mm, name)

            pe.sem_inc(w_used, 4)
            for b in range(4):
                pe.sem_inc(bank_taken[b], 1)

            with pe.Fori(0, DEPTH) as l:
                for u in range(50):
                    pe.wait_ge(w_lo_ready, l * UNITS + u + 5)
                    pe.wait_ge(out_taken, l * OUTS + ring_before(u, OUTS))
                    per_k = (lambda k: pe.wait_ge(h_ready, l * 2 * KT + k + 1)) if u == 0 else None
                    unit(u % 4, main[u % 4], h_hi, h_lo, 0, KT, per_k=per_k).then_inc(w_used, 1)
                    between(l, u)

                for m in range(KT):
                    u = U_BR + m
                    pe.wait_ge(w_lo_ready, l * UNITS + u + 5)
                    for j, (k0, nk) in enumerate(BRANCHES):
                        if m == 0:
                            pe.wait_ge(y_ready, l * 3 + j + 1)
                        bank = use_bank(pe, l, f"branch {m} {j}")
                        mm = unit(u % 4, bank, y_hi, y_lo, k0, nk, wk0=k0)
                        if j < 2:
                            done(mm, f"branch {m} {j}")
                    mm.then_inc(w_used, 1)
                early = KT - 3
                for ms, k0, nk in (((0, 1), 0, early), ((0, 1), early, KT - early), (range(2, KT), 0, KT)):
                    for m in ms:
                        u = U_O + m
                        if k0 == 0:
                            pe.wait_ge(w_lo_ready, l * UNITS + u + 5)
                            pe.wait_ge(out_taken, l * OUTS + O_O + m + 1)
                        per_k = (lambda k: pe.wait_ge(mix_lo_ready, l * KT + k0 + k + 1)) if m == 0 else None
                        mm = unit(u % 4, main[(O_O + m) % 4], mix_hi, mix_lo, k0, nk, wk0=k0, start=k0 == 0,
                                  stop=k0 + nk == KT, per_k=per_k)
                        if k0 + nk == KT:
                            mm.then_inc(w_used, 1)
                for j in range(4):
                    u = U_UP + j
                    pe.wait_ge(w_lo_ready, l * UNITS + u + 5)
                    pe.wait_ge(out_taken, l * OUTS + O_UP + j + 1)
                    per_k = (lambda k: pe.wait_ge(h_ready, l * 2 * KT + KT + k + 1)) if j == 0 else None
                    unit(u % 4, main[(O_UP + j) % 4], h_hi, h_lo, 0, KT, per_k=per_k).then_inc(w_used, 1)
                    if j == 0:
                        sum_squares(l, "norm2", 1)
                with pe.Fori(1, FT // 4) as i:
                    for j in range(4):
                        pe.wait_ge(w_lo_ready, l * UNITS + i * 4 + U_UP + j + 5)
                        pe.wait_ge(out_taken, l * OUTS + i * 4 + O_UP + j + 1)
                        unit((U_UP + j) % 4, main[(O_UP + j) % 4], h_hi, h_lo, 0, KT).then_inc(w_used, 1)
                with pe.Fori(0, 2) as i:
                    for mp in range(2):
                        for kc in range(4):
                            for h in range(2):
                                n = mp * 8 + kc * 2 + h
                                m = mp * 2 + h
                                pe.wait_ge(w_lo_ready, l * UNITS + i * 16 + U_DN + n + 5)
                                if kc == 0:
                                    pe.wait_ge(out_taken, l * OUTS + i * 4 + O_DN + m + 1)
                                if h == 0:
                                    pe.wait_ge(a_ready, l * FT + kc * KT + KT + 4)
                                unit((U_DN + n) % 4, main[(O_DN + m) % 4], a_hi, a_lo, kc * KT, KT,
                                     start=kc == 0, stop=kc == 3).then_inc(w_used, 1)
            sum_squares(DEPTH, "norm1", 0)

        @block.scalar
        def _(act):
            def split_hi(l, u, k=KT, need=None, landed=None):
                n = 33 - (u // 2) % 2
                if isinstance(u, int) and u == 0:
                    act.wait_ge(first_landed, l * 16 + 16)
                else:
                    act.wait_ge(raw_landed[(u // 2) % 2], (l * n + u // 4 + 1) * 16 if landed is None else landed)
                act.wait_ge(w_used, l * UNITS + ring_before(u, UNITS) if need is None else need)
                act.activation(w_hi[:, u % 4, 0:k, :], raw_of(u, k), ACT.Copy).then_inc(w_hi_ready, 1)

            def norm_hi(l, n, k):
                x_ready(act, l, n, k)
                g = (C_G1, C_G2, C_G1)[n]
                act.activation(h_hi[:, k, :], x[:, k, :], ACT.Copy, scale=cur[:, g + k:g + k + 1]).then_inc(h_hi_ready, 1)

            def norm_std(l, n):
                name = ("norm1", "norm2")[n]
                bank = take(act, l, name)
                act.activation(std[:, :], bank[:, 0:TOK], ACT.Sqrt, bias=eps[:, 0:1],
                               scale=1.0 / D_MODEL).then_inc(std_ready, 1)
                act.wait_ge(std_ready, l * 2 + n + 1)
                act.sem_inc(bank_taken[TURN[name] % 4], 1)

            def copy_bank(l, name, dst, src_of, signal):
                bank = take(act, l, name)
                act.activation(dst, src_of(bank), ACT.Copy).then_inc(signal, 1)

            act.wait_ge(lb_ready, 1)
            act.activation(lb_tmp[:, 1:1 + DEPTH, :], lb_tmp[:, 1:1 + DEPTH, :], ACT.Exp).then_inc(lb_exp, 1)
            act.wait_ge(setup_done, 1)
            act.wait_ge(gain_in, 16)
            for k in range(KT - 2):
                act.wait_ge(x_in[k // (KT // 2)], 16)
                act.activation(h_hi[:, k, :], x[:, k, :], ACT.Copy, scale=cur[:, C_G1 + k:C_G1 + k + 1])\
                   .then_inc(h_hi_ready, 1)
            act.dma_start(consts[:, :], io["consts"]).then_inc(consts_in, 16)
            act.dma_start(levels[:, :], io["levels"]).then_inc(levels_in, 16)
            act.dma_start(bands[:, :], io["bands"]).then_inc(bands_in, 16)
            with act.Fori(0, DEPTH) as l:
                step, check_steps = stepper(act, act_step, l, ACT_STEPS)

                def freed(name, signal, value):
                    act.wait_ge(signal, value)
                    act.sem_inc(bank_taken[TURN[name] % 4], 1)

                split_hi(l, 0)
                for k in (KT - 2, KT - 1):
                    norm_hi(l, 0, k)
                for u in range(1, 4):
                    split_hi(l, u)
                act.wait_ge(layer_params, l + 1)
                norm_std(l, 0)
                for u in range(50):
                    if u == 2:
                        z_ready(act, l, CT_CF + 1)
                        step(act.activation(kg[:, :, :], z[:, CT_CF:CT_CF + 2, :], ACT.Sigmoid, scale=-1.0))
                        act.activation(z[:, CT_CF:CT_CF + 2, :], z[:, CT_CF:CT_CF + 2, :], ACT.Sigmoid)\
                           .then_inc(sigmoids, 1)
                    if u == 8:
                        z_ready(act, l, CT_CO + 1)
                        act.activation(o_c[:, :, :], z[:, CT_CO:CT_CO + 2, :], ACT.Sigmoid).then_inc(sigmoids, 1)
                    if u == 7:
                        copy_bank(l, "values T", v_tm[:, :, :, :].rearrange("p t h c -> p (t h c)"),
                                  lambda b: b[:, :], v_tm_ready)
                        freed("values T", v_tm_ready, l + 1)
                        copy_bank(l, "sample values T", v_s[:, :, :].rearrange("p h c -> p (h c)"),
                                  lambda b: b[0:SAMPLES, 0:2 * P], v_s_ready)
                        freed("sample values T", v_s_ready, l + 1)
                    if u == 16:
                        for h in range(2):
                            copy_bank(l, f"level 8 {h}", att_far[:, h, :, :].rearrange("p a c -> p (a c)"),
                                      lambda b: b[:, 0:2 * P], far_ready)
                            freed(f"level 8 {h}", far_ready, 2 * l + h + 1)
                    if u == 18:
                        copy_bank(l, "decayed keys T", k_tm[:, :, :, :].rearrange("p t h c -> p (t h c)"),
                                  lambda b: b[:, :], k_tm_ready)
                        freed("decayed keys T", k_tm_ready, l + 1)
                    if u == 19:
                        act.wait_ge(states_stored, l * STATE_STORES * 16 + 16)
                        copy_bank(l, "state", state_p[:, :, :].rearrange("p h c -> p (h c)"),
                                  lambda b: b[:, 0:2 * HD], state_p_ready)
                        freed("state", state_p_ready, l + 1)
                    if u == 25:
                        for hp in range(2):
                            copy = f"head norm {hp}"
                            bank = take(act, l, copy)
                            act.activation(z[:, CT_CI + hp, :], bank[:, 0:TOK], ACT.Sqrt, bias=eps[:, 0:1])\
                               .then_inc(o_std, 1)
                            freed(copy, o_std, 2 * l + hp + 1)
                    for at, g in ((21, 0), (21, 1), (22, 2)):
                        if u == at:
                            if g == 0:
                                act.wait_ge(stored, l * STORES * 16 + 16)
                            copy_bank(l, f"kv T {g}", kv_tm[:, :, g, :, :],
                                      lambda b: b[:, :].rearrange("p (t k c) -> p t k c", t=2, k=2), kv_tm_ready)
                            freed(f"kv T {g}", kv_tm_ready, NG * l + g + 1)
                    if u == 23:
                        for i, gs in ((0, slice(0, 2)), (1, slice(2, 3))):
                            n = 2 * P * (gs.stop - gs.start)
                            copy_bank(l, f"sample kv T {i}", kv_s[:, gs, :, :].rearrange("p g k c -> p (g k c)"),
                                      lambda b: b[0:SAMPLES, 0:n], kv_s_ready)
                            freed(f"sample kv T {i}", kv_s_ready, 2 * l + i + 1)
                    if u == 24:
                        copy_bank(l, "sample q T", q_s[:, :, :].rearrange("p g c -> p (g c)"),
                                  lambda b: b[0:SAMPLES, 0:NG * P], q_s_ready)
                        freed("sample q T", q_s_ready, l + 1)
                    for h in range(2):
                        if u == 27 + 7 * h:
                            act.wait_ge(maxed, l * 2 + h + 1)
                            step(act.activation(probs[:, 0:NG * P], probs[:, 0:NG * P], ACT.Exp,
                                                bias=stat[:, h, 0:1], accum_out=stat[:, h, 2:3]))
                            act.activation(probs[:, NG * P:9 * P], probs[:, NG * P:9 * P], ACT.Exp,
                                           bias=stat[:, h, 1:2], accum_out=stat[:, h, 3:4]).then_inc(exped, 1)
                        if u == 31 + 7 * h:
                            for j in range(3):
                                nb = min(4, 9 - 4 * j)
                                if h == 1 and j == 0:
                                    take(act, l, "attend 0")
                                copy_bank(l, f"probs T {h} {j}",
                                          probs_t[:, 4 * j:4 * j + nb, :].rearrange("p b c -> p (b c)"),
                                          lambda b: b[:, 0:nb * P], probs_t_ready)
                                freed(f"probs T {h} {j}", probs_t_ready, l * 6 + h * 3 + j + 1)
                    if u == 42:
                        act.wait_ge(s_rows_ready, l + 1)
                        act.activation(s_rows[:, :], s_rows[:, :], ACT.Exp, bias=s_stat[:, 0:1],
                                       accum_out=s_stat[:, 1:2]).then_inc(s_exped, 1)
                    if u == 46:
                        act.wait_ge(yb_ready, l + 1)
                        act.activation(y_hi[:, 1:4, :], z[:, CT_GB:CT_GB + 3, :], ACT.Copy).then_inc(y_hi_ready, 1)
                        act.wait_ge(yc_ready, 2 * l + 2)
                        act.activation(y_hi[:, 4:6, :], o_c[:, :, :], ACT.Copy).then_inc(y_hi_ready, 1)
                    ready = range(5 * (u - 43), min(5 * (u - 42), u - 25)) if 43 <= u < 48 else (u - 26,) if u >= 48 else ()
                    for g in ready:
                        act.wait_ge(out_taken, l * OUTS + 4 + 26 + g + 1)
                        act.activation(gates[:, g, :], gates[:, g, :], ACT.Sigmoid,
                                       bias=cur[:, C_BG + g:C_BG + g + 1]).then_inc(gates_ready, 1)
                    if u == 49:
                        act.wait_ge(ya_ready, l * 3 + 3)
                        act.activation(y_hi[:, 0, :], y_a[:, :], ACT.Copy).then_inc(y_hi_ready, 1)
                    split_hi(l, u + 4, BT if u + 4 >= U_BR else KT)

                for m in range(KT):
                    u = U_BR + m
                    split_hi(l, u + 4, BT if u + 4 < U_O else KT)
                    act.wait_ge(mix_ready, l * KT + m + 1)
                    act.activation(mix_hi[:, m, :], mix[:, m % 2, :], ACT.Copy).then_inc(mix_hi_ready, 1)
                for m in range(KT):
                    norm_hi(l, 1, m)
                    split_hi(l, U_O + m + 4)
                norm_std(l, 1)
                with act.Fori(0, FT // 4) as i:
                    for j in range(4):
                        act.wait_ge(out_taken, l * OUTS + i * 4 + 4 + O_UP + j + 1)
                        act.wait_ge(a_ready, l * FT + i * 4 + j + 1)
                        act.activation(a_full[:, j, :], u_relu[:, j, :], ACT.Square).then_inc(u_used, 1)
                        act.wait_ge(u_used, l * FT + i * 4 + j + 5)
                        act.activation(a_hi[:, bass.ds(i * 4 + j, 1), :].rearrange("p a t -> p (a t)"),
                                       a_full[:, j, :], ACT.Copy).then_inc(a_hi_ready, 1)
                        v = U_UP + j + 4
                        split_hi(l, v, need=l * UNITS + i * 4 + v + 1,
                                 landed=(l * (33 - (v // 2) % 2) + i + v // 4 + 1) * 16)
                for u in range(U_DN, UNITS):
                    if u + 4 < UNITS:
                        split_hi(l, u + 4)
                    n = u - U_DN
                    if n % 8 >= 6 and n < FT - 2:
                        norm_hi(l, 2, n // 8 * 2 + n % 2)
                check_steps()
            norm_std(DEPTH, 0)

        @block.vector
        def _(dve):
            def split_lo(l, u, k=KT, ready=None):
                dve.wait_ge(w_hi_ready, l * UNITS + u + 1 if ready is None else ready)
                dve.tensor_tensor(w_lo[:, u % 4, 0:k, :], raw_of(u, k), w_hi[:, u % 4, 0:k, :].bitcast(F32),
                                  ALU.subtract).then_inc(w_lo_ready, 1)

            def norm_lo(l, n, k):
                g = (C_G1, C_G2, C_G1)[n]
                dve.wait_ge(h_hi_ready, l * 2 * KT + n * KT + k + 1)
                dve.scalar_tensor_tensor(h_lo[:, k, :], x[:, k, :], cur[:, g + k:g + k + 1],
                                         h_hi[:, k, :].bitcast(F32), ALU.mult, ALU.subtract).then_inc(h_ready, 1)

            def last_tile(l):
                dve.wait_ge(w_used, l * UNITS + 4)
                dve.tensor_tensor(x[:, KT - 1, :], main[LAST_BANK][:, 0:TOK], x[:, KT - 1, :], ALU.add)\
                   .then_inc(out_taken, 1)

            def evacuate(l, u):
                unit_done(dve, l, u)
                ct = CT_OF_UNIT[u]
                dst = z[:, ct, :] if ct < CT_GATE else gates[:, ct - CT_GATE, :]
                dve.tensor_tensor(dst, main[u % 4][:, 0:TOK], rstd[:, :], ALU.mult).then_inc(out_taken, 1)

            dve.memset(zeros[:, :], 0.0)
            dve.memset(conv_in[:, :, 0:2], 0.0)
            dve.memset(eps[:, :], EPS).then_inc(setup_done, 1)
            dve.sem_inc(w_lo_ready, 4)
            dve.sem_inc(a_ready, 4)
            dve.wait_ge(hlb_in, 16)
            dve.tensor_tensor(lb_tmp[:, 0, :], hlb[:, 0, :], hlb[:, 1, :], ALU.max).then_inc(lb_step, 1)
            dve.wait_ge(lb_step, 1)
            for d in range(DEPTH):
                ins = dve.tensor_tensor(lb_tmp[:, 1 + d, :], hlb[:, d, :], lb_tmp[:, 0, :], ALU.subtract)
            ins.then_inc(lb_ready, 1)
            dve.wait_ge(lb_exp, 1)
            dve.tensor_tensor(lb_tmp[:, 3, :], lb_tmp[:, 1, :], lb_tmp[:, 2, :], ALU.add).then_inc(lb_step, 1)
            dve.wait_ge(lb_step, 2)
            dve.reciprocal(lb_tmp[:, 4, :], lb_tmp[:, 3, :]).then_inc(lb_step, 1)
            dve.wait_ge(lb_step, 3)
            for d in range(DEPTH):
                ins = dve.tensor_tensor(lb_tmp[:, 1 + d, :], lb_tmp[:, 1 + d, :], lb_tmp[:, 4, :], ALU.mult)
            ins.then_inc(lb_step, 1)
            dve.wait_ge(lb_step, 4)
            dve.tensor_tensor(lb_tmp[:, 5, :], lb_tmp[:, 1, :], lb_tmp[:, 1, :], ALU.subtract)
            dve.tensor_tensor(lb_tmp[:, 3, :], lb_tmp[:, 1, :], lb_tmp[:, 2, :], ALU.add).then_inc(lb_step, 1)
            dve.wait_ge(lb_step, 5)
            dve.tensor_tensor(lb_tmp[:, 6, :], lb_tmp[:, 3, :], lb_tmp[:, 1, :], ALU.subtract).then_inc(lb_step, 1)
            dve.wait_ge(lb_step, 6)
            for d in range(DEPTH):
                dve.tensor_scalar(par[:, d, C_LB:C_LB + 2], lb_tmp[:, 5 + d, :], LB_FLOOR, None, ALU.max)
                ins = dve.tensor_scalar(par[:, d, C_OM:C_OM + 2], lb_tmp[:, 5 + d, :], -1.0, 1.0, ALU.mult, ALU.add)
            ins.then_inc(lb_step, 1)
            dve.wait_ge(lb_step, 7)

            for k in range(KT - 2):
                norm_lo(0, 0, k)
            dve.wait_ge(x_in[0], 16)
            dve.wait_ge(x_in[1], 16)
            dve.memset(main[LAST_BANK][:, 0:TOK], 0.0).then_inc(bank_cleared, 1)
            dve.wait_ge(bank_cleared, 1)
            dve.sem_inc(out_taken, 3)
            dve.wait_ge(params_in, 16)
            with dve.Fori(0, DEPTH) as l:
                step, check_steps = stepper(dve, dve_step, l, DVE_STEPS)

                def norm_inverse(n):
                    dve.wait_ge(std_ready, l * 2 + n + 1)
                    step(dve.reciprocal(rstd[:, :], std[:, :]))

                def mask_level(i):
                    if i == 0:
                        dve.wait_ge(levels_in, 16)
                        dve.wait_ge(att_clear, l + 1)
                    for h in range(2):
                        name = f"level {i} {h}"
                        bank = take(dve, l, name)
                        wait_ends(dve)
                        if i:
                            half = LEVELS[i - 1]
                            n, c = HALF // half, P + (i - 1) * HALF
                            dst = att[:, h, :, :].rearrange("p a (n s t) -> p a n s t", s=2, t=half)[:, :, :, 1, :]
                            mask = levels[:, c:c + HALF].rearrange("p (n t) -> p n t", n=n)
                            src = bank[:, 0:4 * HALF].rearrange("p (a n t) -> p a n t", a=4, n=n)
                            mask = mask.unsqueeze(1).to_broadcast([P, 4, n, half])
                        else:
                            dst, mask = att[:, h, :, :], levels[:, 0:P].unsqueeze(1).to_broadcast([P, 4, P])
                            src = bank[:, :].rearrange("p (a c) -> p a c", a=4)
                        ins = dve.copy_predicated(dst, mask.bitcast(U32), src)
                        ins.then_inc(masked, 1)
                        dve.wait_ge(masked, l * 16 + 2 * i + h + 1)
                        dve.sem_inc(bank_taken[TURN[name] % 4], 1)

                def mask_scores(h):
                    if h == 0:
                        dve.wait_ge(bands_in, 16)
                    if h == 1:
                        take(dve, l, "probs T 0 2")
                    at = 0
                    for j, n in enumerate((NG * P, 2 * PROMPT, PROMPT)):
                        bank = take(dve, l, f"scores {h} {j}")
                        taken_step(dve.scalar_tensor_tensor(probs[:, at:at + n], bank[:, 0:n], SCALE,
                                                            bands[:, at:at + n], ALU.mult, ALU.add),
                                   f"scores {h} {j}")
                        at += n
                    dve.reduce_max(stat[:, h, 0:1], probs[:, 0:NG * P], AX_X, negate=True)
                    dve.reduce_max(stat[:, h, 1:2], probs[:, NG * P:9 * P], AX_X, negate=True).then_inc(maxed, 1)

                def taken_step(ins, name):
                    step(ins)
                    dve.sem_inc(bank_taken[TURN[name] % 4], 1)

                def normalise(h):
                    dve.wait_ge(exped, l * 2 + h + 1)
                    step(dve.reciprocal(stat[:, h, 0:2], stat[:, h, 2:4]))
                    dve.tensor_scalar(probs[:, 0:NG * P], probs[:, 0:NG * P], stat[:, h, 0:1], None, ALU.mult)
                    dve.tensor_scalar(probs[:, NG * P:9 * P], probs[:, NG * P:9 * P], stat[:, h, 1:2], None,
                                      ALU.mult).then_inc(probs_ready, 1)

                def sample_scores(b):
                    dve.wait_ge(q_rows_in[b // (SAMPLES // 2)], l * 16 + 16)
                    if b == 0:
                        dve.wait_ge(keys_in, l * NG * 16 + NG * 16)
                    full = [g for g, (win, dil) in enumerate(GROUPS) if PAST // dil >= BAND]
                    parts = [(slice(0, len(full)), BAND)] + [(slice(g, g + 1), PAST // GROUPS[g][1])
                                                             for g in range(len(full), NG)]
                    for gs, n in parts:
                        ins = dve.tensor_tensor(k_cache[0:n, b, gs, :], k_cache[0:n, b, gs, :], q_rows[0:n, b, gs, :],
                                                ALU.mult)
                    step(ins)
                    for gs, n in parts:
                        ins = dve.tensor_reduce(sc[0:n, gs, b, :],
                                                k_cache[0:n, b, gs, :].rearrange("p g (h d) -> p g h d", h=2),
                                                AX_X, ALU.add)
                    if b == SAMPLES - 1:
                        for gs, n in parts:
                            if n < BAND:
                                ins = dve.memset(sc[n:BAND, gs, :, :], NEG / SCALE)
                        ins.then_inc(s_scored, 1)

                def convolve(tap):
                    if tap == 2:
                        dve.wait_ge(conv_in_ready, l + 1)
                        dve.wait_ge(state_in, (l * 5 + 5) * 16)
                    for j in range(3):
                        w = cur[:, C_CW + tap * 3 + j:C_CW + tap * 3 + j + 1]
                        acc, acc_s = z[:, CT_GC + j, 0:PROMPT], z[:, CT_GC + j, PROMPT:TOK]
                        src = conv_in[:, j, tap:tap + PROMPT]
                        src_s = conv_u[:, j, :] if tap == 2 else conv_s[:, j, :, tap]
                        if tap == 2:
                            dve.tensor_scalar(acc, src, w, None, ALU.mult)
                            ins = dve.tensor_scalar(acc_s, src_s, w, None, ALU.mult)
                        else:
                            dve.scalar_tensor_tensor(acc, src, w, acc, ALU.mult, ALU.add)
                            ins = dve.scalar_tensor_tensor(acc_s, src_s, w, acc_s, ALU.mult, ALU.add)
                    if tap:
                        step(ins)
                    else:
                        ins.then_inc(conv_out, 1)

                split_lo(l, 0)
                last_tile(l)
                for k in (KT - 2, KT - 1):
                    norm_lo(l, 0, k)
                dve.wait_ge(h_ready, l * 2 * KT + KT)
                step(dve.tensor_copy(cur[:, :], par[:, bass.ds(l, 1), :].rearrange("p a c -> p (a c)")))
                dve.sem_inc(layer_params, 1)
                for u in range(1, 3):
                    split_lo(l, u)
                norm_inverse(0)
                for u in range(50):
                    if u == 26:
                        dve.wait_ge(state_s_ready, l + 1)
                        dve.wait_ge(roped, l + 1)
                    evacuate(l, u)
                    if u == 3:
                        dve.wait_ge(sigmoids, 2 * l + 1)
                        for hp in range(2):
                            lb, om = cur[:, C_LB + hp:C_LB + hp + 1], cur[:, C_OM + hp:C_OM + hp + 1]
                            sg = z[:, CT_CF + hp, :]
                            dve.tensor_scalar(cum_f[:, hp, :], sg[:, 0:PROMPT], om, lb, ALU.mult, ALU.add)
                            dve.tensor_scalar(f_s[:, hp, :], sg[:, PROMPT:TOK], om, lb, ALU.mult, ALU.add)
                            ins = dve.tensor_scalar(kg[:, hp, :], kg[:, hp, :], om, None, ALU.mult)
                        step(ins)
                        dve.sem_inc(decays, 1)
                        dve.sem_inc(kg_ready, 1)
                    if 8 <= u < 16:
                        mask_level(u - 8)
                    if u == 17:
                        for i4 in range(2):
                            bank = take(dve, l, f"sample values {i4}")
                            b4 = slice(i4 * 4, i4 * 4 + 4)
                            ks = kg[:, :, PROMPT + i4 * 4:PROMPT + i4 * 4 + 4].rearrange("p h b -> p b h")
                            ins = dve.tensor_tensor(
                                kv_outer[:, b4, :, :],
                                bank[:, :].rearrange("p (b h v) -> p b h v", b=4, h=2),
                                ks.unsqueeze(3).to_broadcast([P, 4, 2, HD]), ALU.mult)
                            ins.then_inc(outer_ready, 1)
                            dve.wait_ge(outer_ready, l * 2 + i4 + 1)
                            dve.sem_inc(bank_taken[TURN[f"sample values {i4}"] % 4], 1)
                    if u == 18:
                        dve.wait_ge(halves_swapped, (l * 4 + 4) * 16)
                        dve.tensor_tensor(swapped_qk, swapped_qk, sin.unsqueeze(1).to_broadcast([P, 6, TOK]),
                                          ALU.mult).then_inc(sin_ready, 1)
                    if u == 19:
                        bank = take(dve, l, "recurrence")
                        dve.wait_ge(silu_ready, l + 1)
                        dve.tensor_copy(o_c[:, :, 0:PROMPT], bank[:, :].rearrange("p (h t) -> p h t", h=2))\
                           .then_inc(o_ready, 1)
                        dve.wait_ge(o_ready, 2 * l + 1)
                        dve.sem_inc(bank_taken[TURN["recurrence"] % 4], 1)
                    if u == 23:
                        bank = take(dve, l, "sample recurrence")
                        dve.tensor_copy(o_c[:, :, PROMPT:TOK],
                                        bank[:, 0:2 * SAMPLES].rearrange("p (h t) -> p h t", h=2)).then_inc(o_ready, 1)
                        dve.wait_ge(o_ready, 2 * l + 2)
                        dve.sem_inc(bank_taken[TURN["sample recurrence"] % 4], 1)
                        dve.sem_inc(state_s_used, 1)
                    if u in (27, 29):
                        hp = (u - 27) // 2
                        dve.wait_ge(o_std, 2 * l + hp + 1)
                        dve.reciprocal(z[:, CT_CI + hp, :], z[:, CT_CI + hp, :]).then_inc(o_inv, 1)
                    for at, tap in ((31, 2), (41, 1), (44, 0)):
                        if u == at:
                            convolve(tap)
                    if u == 32:
                        dve.wait_ge(o_scaled, l + 1)
                        for hp in range(2):
                            dve.scalar_tensor_tensor(o_c[:, hp, :], o_c[:, hp, :],
                                                     cur[:, C_HN + hp:C_HN + hp + 1], z[:, CT_CO + hp, :],
                                                     ALU.mult, ALU.mult).then_inc(yc_ready, 1)
                    for h in range(2):
                        if u == 26 + 7 * h:
                            mask_scores(h)
                        if u == 28 + 7 * h:
                            normalise(h)
                        if u == 33 + 7 * h:
                            bank = take(dve, l, f"attend {h}")
                            rows = slice(h * HD, (h + 1) * HD)
                            dve.tensor_copy(y_a[rows, 0:PROMPT], bank[rows, 0:PROMPT]).then_inc(ya_ready, 1)
                            dve.wait_ge(ya_ready, 3 * l + h + 1)
                            dve.sem_inc(bank_taken[TURN[f"attend {h}"] % 4], 1)
                    for b, at in enumerate((30, 32, 34, 36, 37, 38, 39, 40)):
                        if u == at:
                            sample_scores(b)
                    if u == 42:
                        bank = take(dve, l, "sample scores T")
                        dve.tensor_scalar(s_rows[:, 0:NG * P], bank[0:16, 0:NG * P], SCALE, None, ALU.mult)
                        step(dve.scalar_tensor_tensor(
                            new_sc[:, :, :].rearrange("p g b -> p (g b)"), bank[0:16, NG * P:NG * P + NG * SAMPLES],
                            SCALE, diag, ALU.mult, ALU.mult))
                        dve.sem_inc(bank_taken[TURN["sample scores T"] % 4], 1)
                        step(dve.reduce_sum(s_rows[:, NG * P:NG * P + NG], new_sc[:, :, :], AX_X))
                        dve.reduce_max(s_stat[:, 0:1], s_rows[:, :], AX_X, negate=True).then_inc(s_rows_ready, 1)
                    if u == 43:
                        dve.wait_ge(s_exped, l + 1)
                        step(dve.reciprocal(s_stat[:, 2:3], s_stat[:, 1:2]))
                        step(dve.tensor_scalar(s_rows[:, :], s_rows[:, :], s_stat[:, 2:3], None, ALU.mult))
                        dve.tensor_tensor(new_sc[:, :, :], diag.rearrange("p (g b) -> p g b", g=NG),
                                          s_rows[:, NG * P:NG * P + NG].unsqueeze(2).to_broadcast([16, NG, SAMPLES]),
                                          ALU.mult).then_inc(s_probs, 1)
                    if u == 47:
                        for i, (lo_, n) in enumerate(((1, 3), (4, 2))):
                            dve.wait_ge(y_hi_ready, 3 * l + i + 1)
                            src = z[:, CT_GB:CT_GB + 3, :] if i == 0 else o_c[:, :, :]
                            dve.tensor_tensor(y_lo[:, lo_:lo_ + n, :], src, y_hi[:, lo_:lo_ + n, :].bitcast(F32),
                                              ALU.subtract).then_inc(y_ready, 1)
                    if u == 45:
                        bank = take(dve, l, "sample probs T")
                        step(dve.tensor_copy(pr_s[:, :, :, :].rearrange("p g b h -> p (g b h)"), bank[:, 0:48]))
                        dve.sem_inc(s_probs_t, 1)
                        step(dve.tensor_tensor(new_pv[:, :, :],
                                               bank[:, 64:64 + NG * SAMPLES].rearrange("p (g b) -> p g b", g=NG),
                                               z[:, CT_V:CT_V + NG, PROMPT:TOK], ALU.mult))
                        dve.sem_inc(bank_taken[TURN["sample probs T"] % 4], 1)
                        step(dve.reduce_sum(ya_new[:, :], new_pv[:, :, :].rearrange("p g b -> p b g"), AX_X))
                    if u == 49:
                        bank = take(dve, l, "sample attend")
                        for h in range(2):
                            rows = slice(h * HD, (h + 1) * HD)
                            own = bank[rows, 0:16].rearrange("p (b h) -> p b h", h=2)[:, :, h]
                            ins = dve.tensor_tensor(y_a[rows, PROMPT:TOK], own, ya_new[rows, :], ALU.add)
                        step(ins)
                        dve.sem_inc(bank_taken[TURN["sample attend"] % 4], 1)
                        dve.sem_inc(ya_ready, 1)
                    if u == 49:
                        dve.wait_ge(y_hi_ready, 3 * l + 3)
                        dve.tensor_tensor(y_lo[:, 0, :], y_a[:, :], y_hi[:, 0, :].bitcast(F32), ALU.subtract)\
                           .then_inc(y_ready, 1)
                    split_lo(l, u + 3, BT if u + 3 >= U_BR else KT)

                for m in range(KT):
                    u = U_BR + m
                    if m >= 2:
                        dve.wait_ge(mix_ready, l * KT + m - 1)
                    dve.wait_ge(gates_ready, l * N_GATE + 2 * KT + m + 1)
                    for j in range(3):
                        name = f"branch {m} {j}"
                        if j < 2:
                            bank = take(dve, l, name)
                        else:
                            unit_done(dve, l, u)
                            bank = small[TURN[name] % 4]
                        dve.tensor_tensor(gated[:, m % 2, j, :], bank[:, 0:TOK], gates[:, BRANCH_GATE[j] * KT + m, :], ALU.mult)\
                           .then_inc(bank_taken[TURN[name] % 4], 1)
                    split_lo(l, u + 3, BT if u + 3 < U_O else KT)
                s = (KT - 1) % 2
                for j in range(3):
                    after_taken(dve, l, f"branch {KT - 1} {j}")
                step(dve.tensor_tensor(gated[:, s, 0, :], gated[:, s, 0, :], gated[:, s, 1, :], ALU.add))
                dve.wait_ge(mix_ready, l * KT + KT - 1)
                dve.wait_ge(mix_lo_ready, l * KT + KT - 2)
                dve.tensor_tensor(mix[:, s, :], gated[:, s, 0, :], gated[:, s, 2, :], ALU.add).then_inc(mix_ready, 1)
                dve.wait_ge(mix_hi_ready, l * KT + KT)
                dve.wait_ge(mix_lo_ready, l * KT + KT - 1)
                dve.tensor_tensor(mix_lo[:, KT - 1, :], mix[:, s, :], mix_hi[:, KT - 1, :].bitcast(F32),
                                  ALU.subtract).then_inc(mix_lo_ready, 1)
                for m in range(KT):
                    u = U_O + m
                    unit_done(dve, l, u)
                    dve.tensor_tensor(x[:, m, :], main[(O_O + m) % 4][:, 0:TOK], x[:, m, :], ALU.add)\
                       .then_inc(out_taken, 1)
                    split_lo(l, u + 3)
                    norm_lo(l, 1, m)
                norm_inverse(1)
                wait_ends(dve)
                with dve.Fori(0, FT // 4) as i:
                    for j in range(4):
                        dve.wait_ge(w_used, l * UNITS + i * 4 + 4 + U_UP + j + 1)
                        dve.wait_ge(u_used, l * FT + i * 4 + j + 1)
                        dve.scalar_tensor_tensor(u_relu[:, j, :], main[(O_UP + j) % 4][:, 0:TOK], 0.0, rstd[:, :],
                                                 ALU.max, ALU.mult).then_inc(out_taken, 1)
                        v = U_UP + j + 3
                        split_lo(l, v, ready=l * UNITS + i * 4 + v + 1)
                        dve.wait_ge(a_hi_ready, l * FT + i * 4 + j + 1)
                        at = bass.ds(i * 4 + j, 1)
                        dve.tensor_tensor(a_lo[:, at, :].rearrange("p a t -> p (a t)"), a_full[:, j, :],
                                          a_hi[:, at, :].rearrange("p a t -> p (a t)").bitcast(F32),
                                          ALU.subtract).then_inc(a_ready, 1)
                for n in range(FT):
                    u = U_DN + n
                    if n >= 8 and n % 8 < 2:
                        norm_lo(l, 2, n // 8 * 2 - 2 + n % 2)
                    if n % 8 >= 6 and n < FT - 1:
                        m = n // 8 * 2 + n % 2
                        unit_done(dve, l, u)
                        dve.tensor_tensor(x[:, m, :], main[(O_DN + m) % 4][:, 0:TOK], x[:, m, :], ALU.add)\
                           .then_inc(out_taken, 1)
                    if u + 3 < UNITS:
                        split_lo(l, u + 3)
                check_steps()
            last_tile(DEPTH)
            dve.wait_ge(std_ready, DEPTH * 2 + 1)
            dve.reciprocal(rstd[:, :], std[:, :]).then_inc(lb_step, 1)
            dve.wait_ge(lb_step, 8)
            for k in range(KT):
                dve.scalar_tensor_tensor(x[:, k, :], x[:, k, :], cur[:, C_G1 + k:C_G1 + k + 1], rstd[:, :], ALU.mult,
                                         ALU.mult).then_inc(y_out, 1)

        @block.gpsimd
        def _(pool):
            def squares(step, norm, ready, previous):
                for k in range(KT):
                    ready(k)
                    if k == 0:
                        previous()
                        step(pool.tensor_tensor(sq_sum[:, :], x[:, k, :], x[:, k, :], ALU.mult))
                        continue
                    step(pool.tensor_tensor(sq[:, :], x[:, k, :], x[:, k, :], ALU.mult))
                    ins = pool.tensor_tensor(sq_sum[:, :], sq_sum[:, :], sq[:, :], ALU.add)
                    if k < KT - 1:
                        step(ins)
                ins.then_inc(sq_ready, 1)

            pool_start, _ = stepper(pool, pool_setup, 0, 0)
            squares(pool_start, 0, lambda k: pool.wait_ge(out_taken, 4) if k == KT - 1 else pool.wait_ge(x_in[k // (KT // 2)], 16),
                    lambda: None)
            pool.sem_inc(u_used, 4)
            with pool.Fori(0, DEPTH) as l:
                step, check_steps = stepper(pool, pool_step, l, POOL_STEPS)
                z_ready(pool, l, CT_CQ)
                wait_ends(pool)
                pool.memset(att[:, :, :, :].rearrange("p a b c -> p (a b c)"), 0.0).then_inc(att_clear, 1)
                pool.memset(q_heads[:, :, :, :].rearrange("p a b c -> p (a b c)"), 0.0)
                pool.memset(k_lv[:, :, :, :].rearrange("p a h t -> p (a h t)"), 0.0)
                step(pool.memset(suf_f[:, :, :].rearrange("p a b -> p (a b)"), 1.0))
                pool.wait_ge(decays, l + 1)
                z_ready(pool, l, CT_CQ + 1)
                for i, half in enumerate(LEVELS, 1):
                    if i >= 3:
                        take(pool, l, f"level {i - 2} 1")
                    def halves(t, s, half=half):
                        return t.rearrange("p h (n s t) -> p h n s t", s=2, t=half)[:, :, :, s, :]
                    for hp in range(2):
                        one = slice(hp, hp + 1)
                        pool.tensor_tensor(halves(q_lv[:, i % 2, one, :], 1),
                                           halves(z[:, CT_CQ + hp:CT_CQ + hp + 1, 0:PROMPT], 1),
                                           halves(cum_f[:, one, :], 1), ALU.mult)
                        ins = pool.tensor_tensor(halves(k_lv[:, i % 2, one, :], 0), halves(kg[:, one, 0:PROMPT], 0),
                                                 halves(suf_f[:, one, :], 0), ALU.mult)
                    step(ins)
                    pool.sem_inc(level_ready, 1)
                    suf = suf_f[:, :, :].rearrange("p h (n s t) -> p (h n) s t", s=2, t=half)
                    cum = cum_f[:, :, :].rearrange("p h (n s t) -> p (h n) s t", s=2, t=half)
                    n = PROMPT // half
                    step(pool.tensor_tensor(suf[:, :, 0, :], suf[:, :, 0, :],
                                            cum[:, :, 1, half - 1:half].to_broadcast([P, n, half]), ALU.mult))
                    if i < 8:
                        step(pool.tensor_tensor(cum[:, :, 1, :], cum[:, :, 1, :],
                                                cum[:, :, 0, half - 1:half].to_broadcast([P, n, half]), ALU.mult))
                take(pool, l, "level 7 1")
                pool.tensor_tensor(q_lv[:, 1, :, :], kg[:, :, 0:PROMPT], suf_f[:, :, :], ALU.mult).then_inc(final_keys, 1)
                pool.wait_ge(sigmoids, 2 * l + 2)
                pool.tensor_tensor(z[:, CT_CO:CT_CO + 2, :], z[:, CT_CO:CT_CO + 2, :], o_c[:, :, :], ALU.mult)\
                    .then_inc(silu_ready, 1)
                pool.wait_ge(halves_swapped, (l * 4 + 4) * 16)
                step(pool.tensor_tensor(z[:, CT_Q:CT_V, :], z[:, CT_Q:CT_V, :],
                                        cos.unsqueeze(1).to_broadcast([P, 6, TOK]), ALU.mult))
                pool.wait_ge(sin_ready, l + 1)
                pool.tensor_tensor(z[:, CT_Q:CT_V, :], z[:, CT_Q:CT_V, :], swapped_qk, ALU.add).then_inc(roped, 1)
                pool.wait_ge(state_in, (l * 5 + 5) * 16)
                pool.wait_ge(outer_ready, l * 2 + 2)
                fs = f_s[:, :, :].rearrange("p h b -> p b h").unsqueeze(3).to_broadcast([P, SAMPLES, 2, HD])
                step(pool.tensor_tensor(state_s[:, :, :, :], state_s[:, :, :, :], fs, ALU.mult))
                pool.tensor_tensor(state_s[:, :, :, :], state_s[:, :, :, :], kv_outer, ALU.add)\
                    .then_inc(state_s_ready, 1)
                pool.wait_ge(roped, l + 1)
                for h in range(2):
                    rows = slice(h * HD, (h + 1) * HD)
                    wait_ends(pool)
                    step(pool.tensor_copy(q_heads[rows, :, :, h], z[rows, CT_Q:CT_Q + NG, PROMPT:TOK]))
                pool.sem_inc(q_heads_ready, 1)
                pool.wait_ge(o_ready, 2 * l + 2)
                pool.tensor_tensor(z[:, CT_CF:CT_CF + 2, :], o_c[:, :, :], o_c[:, :, :], ALU.mult).then_inc(o_sq_ready, 1)
                z_ready(pool, l, CT_GC + 2)
                pool.wait_ge(stored, l * STORES * 16 + 16)
                pool.tensor_tensor(conv_in[:, :, 2:2 + PROMPT], z[:, CT_HB:CT_HB + 3, 0:PROMPT],
                                   z[:, CT_GC:CT_GC + 3, 0:PROMPT], ALU.mult)
                step(pool.tensor_tensor(conv_u[:, :, :], z[:, CT_HB:CT_HB + 3, PROMPT:TOK],
                                        z[:, CT_GC:CT_GC + 3, PROMPT:TOK], ALU.mult))
                pool.sem_inc(conv_in_ready, 1)
                pool.tensor_copy(conv_new[:, :, :, 0], conv_s[:, :, :, 1])
                pool.tensor_copy(conv_new[:, :, :, 1], conv_u[:, :, :]).then_inc(conv_new_ready, 1)
                pool.wait_ge(o_inv, 2 * l + 2)
                pool.tensor_tensor(o_c[:, :, :], o_c[:, :, :], z[:, CT_CI:CT_CI + 2, :], ALU.mult).then_inc(o_scaled, 1)
                pool.wait_ge(conv_out, l + 1)
                pool.tensor_tensor(z[:, CT_GB:CT_GB + 3, :], z[:, CT_GB:CT_GB + 3, :], z[:, CT_GC:CT_GC + 3, :],
                                   ALU.mult).then_inc(yb_ready, 1)
                def mix_half(m):
                    pool.wait_ge(mix_hi_ready, l * KT + m + 1)
                    pool.tensor_tensor(mix_lo[:, m, :], mix[:, m % 2, :], mix_hi[:, m, :].bitcast(F32),
                                       ALU.subtract).then_inc(mix_lo_ready, 1)
                for m in range(KT - 1):
                    for j in range(3):
                        after_taken(pool, l, f"branch {m} {j}")
                    if m >= 2:
                        pool.wait_ge(mix_lo_ready, l * KT + m - 1)
                    s = m % 2
                    step(pool.tensor_tensor(gated[:, s, 0, :], gated[:, s, 0, :], gated[:, s, 1, :], ALU.add))
                    pool.tensor_tensor(mix[:, s, :], gated[:, s, 0, :], gated[:, s, 2, :], ALU.add).then_inc(mix_ready, 1)
                    if m:
                        mix_half(m - 1)
                mix_half(KT - 2)
                squares(step, 1, lambda m: x_ready(pool, l, 1, m), lambda: take(pool, l, "norm1"))
                squares(step, 2, lambda m: x_ready(pool, l, 2, m), lambda: take(pool, l, "norm2"))
                check_steps()


def constants():
    c = np.zeros((P, NCONST), np.float32)
    c[:, K_ID:K_ID + P] = np.eye(P)
    c[:, K_ONE:K_ONE + P] = 1.0
    for head in range(2):
        r = slice(head * HD, (head + 1) * HD)
        c[r, K_BLK + head * HD:K_BLK + (head + 1) * HD] = 1.0 / HD
    half = HD // 2
    inv = (np.float32(10000.0) ** (-np.arange(half, dtype=np.float32) / np.float32(half))).astype(np.float32)
    pos = np.concatenate([np.arange(PROMPT), np.full(SAMPLES, PAST)]).astype(np.float32)
    ang = inv[np.arange(P) % half][:, None] * pos[None, :]
    c[:, K_COS:K_COS + TOK] = np.cos(ang.astype(np.float32))
    sign = np.where(np.arange(P) % HD < half, -1.0, 1.0)[:, None]
    c[:, K_SIN:K_SIN + TOK] = np.sin(ang.astype(np.float32)) * sign
    for b in range(SAMPLES):
        for h in range(2):
            for g in range(NG):
                c[b * 2 + h, K_DIAG + g * SAMPLES + b] = 1.0
            c[b * 2 + h, K_HSEL + h * HD:K_HSEL + (h + 1) * HD] = 1.0
    return c


def band_masks():
    out = []
    for q0, n in ((0, P), (P, PROMPT)):
        for win, dil in GROUPS:
            q = q0 + np.arange(P)[:, None]
            k = np.arange(n)[None, :]
            ok = (k <= q) & ((q - k) % dil == 0) & (q - k <= win)
            out.append(np.where(ok, 0.0, NEG))
    return np.concatenate(out, 1).astype(np.float32)


def level_masks():
    s, t = np.arange(P)[:, None], np.arange(P)[None, :]
    out = [s == t]
    for half in LEVELS[:-1]:
        late = (t[0] % (2 * half) >= half).nonzero()[0]
        out.append(((s // (2 * half) == t // (2 * half)) & (s % (2 * half) < half))[:, late])
    return np.concatenate(out, 1).astype(np.float32)


def kernel(x_prompt, x_sample, cache_kv_w128, cache_kv_w512, cache_kv_w2048, state_conv, state_hgrn,
           w_in, b_gate, norm1, conv_w, hgrn_lb, hgrn_norm, w_pa, w_pb, w_pc, w_o, norm2, w_up, w_down, norm_f):
    import concourse.bacc as bacc
    from concourse.bass_utils import run_bass_kernel_spmd

    A = np.ascontiguousarray

    def columns(a):
        a = np.asarray(a)
        return a.reshape(DEPTH, -1, P).transpose(2, 0, 1)

    cw = np.asarray(conv_w).reshape(DEPTH, 3 * 3 * P)
    arrays = {
        "consts": constants(),
        "bands": band_masks(),
        "levels": level_masks(),
        "gain0": A(columns(norm1)[:, 0]),
        "params": A(np.concatenate([columns(np.concatenate([np.asarray(norm1)[1:], np.asarray(norm_f)[None]])),
                                    columns(norm2), columns(b_gate), columns(cw),
                                    columns(hgrn_norm)], 2)),
        "hlb": A(columns(hgrn_lb)),
        "xT": A(np.concatenate([np.asarray(x_prompt)[0], np.asarray(x_sample)[:, 0]], 0).T),
        "w_in": A(w_in), "w_o": A(w_o), "w_up": A(w_up), "w_down": A(w_down),
        "w_br": A(np.concatenate([np.asarray(w_pa), np.asarray(w_pb), np.asarray(w_pc)], 1)),
        "state_convT": A(np.asarray(state_conv).reshape(DEPTH, SAMPLES, 2, 3, P).transpose(0, 4, 3, 1, 2)),
        "state_hgrn": A(state_hgrn),
    }
    for g, c in enumerate((cache_kv_w128, cache_kv_w512, cache_kv_w2048)):
        arrays[f"cache{g}"] = A(np.asarray(c).reshape(DEPTH, SAMPLES, -1, ROW))
    outs = {"yT": (D_MODEL, TOK), "convpT": (DEPTH, P, 3, 2), "convsT": (DEPTH, P, 3, SAMPLES, 2),
            "hgp": (DEPTH, 1, 4, HD, HD), "hgs": (DEPTH, SAMPLES, 4, HD, HD)}
    for g, (win, _) in enumerate(GROUPS):
        outs[f"kvp{g}"] = (DEPTH, 1, win, ROW)
        outs[f"kvs{g}"] = (DEPTH, SAMPLES, win, ROW)

    nc = bacc.Bacc("TRN2", target_bir_lowering=False, num_devices=1)
    io = {n: nc.dram_tensor(f"in_{n}", a.shape, mybir.dt.from_np(a.dtype), kind="ExternalInput").ap()
          for n, a in arrays.items()}
    io |= {n: nc.dram_tensor(f"out_{n}", s, F32, kind="ExternalOutput").ap() for n, s in outs.items()}
    io["q_scratch"] = nc.dram_tensor("q_scratch", (SAMPLES, NG * P), F32, kind="Internal").ap()
    trunk(nc, io)
    r = run_bass_kernel_spmd(nc, [{f"in_{n}": a for n, a in arrays.items()}], core_ids=[0]).results[0]
    r = {n: r[f"out_{n}"] for n in outs}

    y = r["yT"].T
    kvp = [r[f"kvp{g}"].reshape(DEPTH, 1, win, 2, 2, HD) for g, (win, _) in enumerate(GROUPS)]
    kvs = [r[f"kvs{g}"].reshape(DEPTH, SAMPLES, win, 2, 2, HD) for g, (win, _) in enumerate(GROUPS)]
    conv_p = r["convpT"].transpose(0, 3, 2, 1).reshape(DEPTH, 1, 2, 3 * P)
    conv_s = r["convsT"].transpose(0, 3, 4, 2, 1).reshape(DEPTH, SAMPLES, 2, 3 * P)
    return (A(y[None, :PROMPT]), A(y[PROMPT:, None]), *kvp, A(conv_p), r["hgp"], *kvs, A(conv_s), r["hgs"])
```
